# Optimizing a Trainium2 kernel written in Bass

```python
import jax, jax.numpy as jnp
from jax import lax
import numpy as np

D_MODEL = 1024
BATCH = 1
SEQ = 256
DEPTH = 1

GRID_W = 64
CTX_LEN = 256
ATTN_WIDTH = 512
N_HEADS = 8
N_KV_HEADS = 2
HEAD_DIM = ATTN_WIDTH // N_HEADS
KV_REP = N_HEADS // N_KV_HEADS
KV_WIDTH = N_KV_HEADS * HEAD_DIM
CONV_WIDTH = D_MODEL - ATTN_WIDTH
CONV_HEADS = 8
CONV_K = 3
MIX_WIDTH = ATTN_WIDTH + CONV_WIDTH
IN_COLS = ATTN_WIDTH + 2 * KV_WIDTH + 3 * CONV_WIDTH
ROPE_THETA = 10000.0
ROPE_AXIS_DIM = HEAD_DIM // 2
ROPE_FREQS = ROPE_AXIS_DIM // 2
Q_BLOCK = 128
N_GROUPS = 4
EXPERTS_PER_GROUP = 8
N_EXPERTS = N_GROUPS * EXPERTS_PER_GROUP
TOP_K = 2
D_EXPERT = 768
MOE_BLOCK = 128
N_MOD = 6
EPS = 1e-6


def rms_norm(x, g):
    xf = x.astype(jnp.float32)
    y = xf * lax.rsqrt(jnp.mean(xf * xf, axis=-1, keepdims=True) + EPS)
    return (y * g.astype(jnp.float32)).astype(x.dtype)

def head_rms(x, g, n_heads):
    xs = x.reshape(*x.shape[:-1], n_heads, -1)
    return rms_norm(xs, g.reshape(n_heads, -1)).reshape(x.shape)

def modulation(cond, w_mod, b_mod):
    mod = jax.nn.silu(cond) @ w_mod + b_mod
    return jnp.split(mod[..., None, :], N_MOD, axis=-1)

def axial_rope_tables(n_tokens, dtype):
    rows = n_tokens // GRID_W
    row_idx = jnp.repeat(jnp.arange(rows, dtype=jnp.float32), GRID_W)
    col_idx = jnp.tile(jnp.arange(GRID_W, dtype=jnp.float32), rows)
    inv_freq = ROPE_THETA ** (-jnp.arange(0, ROPE_AXIS_DIM, 2, dtype=jnp.float32) / ROPE_AXIS_DIM)
    ang = jnp.stack([row_idx[:, None] * inv_freq, col_idx[:, None] * inv_freq], axis=1)
    return jnp.cos(ang).astype(dtype), jnp.sin(ang).astype(dtype)

def apply_axial_rope(x, cos, sin):
    xs = x.reshape(*x.shape[:-1], 2, 2, ROPE_FREQS)
    x1, x2 = xs[..., 0, :], xs[..., 1, :]
    c, s = cos[:, None], sin[:, None]
    return jnp.stack([x1 * c - x2 * s, x1 * s + x2 * c], axis=-2).reshape(x.shape)

def in_proj(h, w_in, q_g, k_g):
    z = h @ w_in
    b, s = h.shape[:2]
    cuts = [ATTN_WIDTH, ATTN_WIDTH + KV_WIDTH, ATTN_WIDTH + 2 * KV_WIDTH,
            ATTN_WIDTH + 2 * KV_WIDTH + CONV_WIDTH, ATTN_WIDTH + 2 * KV_WIDTH + 2 * CONV_WIDTH]
    q, k, v, gb, gc, u = jnp.split(z, cuts, axis=-1)
    q = rms_norm(q.reshape(b, s, N_HEADS, HEAD_DIM), q_g)
    k = rms_norm(k.reshape(b, s, N_KV_HEADS, HEAD_DIM), k_g)
    v = v.reshape(b, s, N_KV_HEADS, HEAD_DIM)
    return q, k, v, gb, gc, u

def attend(q, k, v):
    s = jnp.einsum('bqgrd,bkgd->bgrqk', q, k, preferred_element_type=jnp.float32) * (HEAD_DIM ** -0.5)
    p = jax.nn.softmax(s, axis=-1).astype(v.dtype)
    return jnp.einsum('bgrqk,bkgd->bqgrd', p, v)

def latent_attention(q, k_all, v_all):
    b, s = q.shape[:2]
    nb = s // Q_BLOCK
    qb = q.reshape(b, nb, Q_BLOCK, N_KV_HEADS, KV_REP, HEAD_DIM).transpose(1, 0, 2, 3, 4, 5)
    ob = lax.map(lambda qi: attend(qi, k_all, v_all), qb)
    return ob.transpose(1, 0, 2, 3, 4, 5).reshape(b, s, ATTN_WIDTH)

def short_conv(gb, gc, u, conv_w):
    v = gc * u
    vp = jnp.pad(v, ((0, 0), (1, 1), (0, 0)))
    y = conv_w[0] * vp[:, :-2] + conv_w[1] * vp[:, 1:-1] + conv_w[2] * vp[:, 2:]
    return gb * y

def merge_out(a, cv, attn_g, conv_g, w_out):
    return jnp.concatenate([head_rms(a, attn_g, N_HEADS), head_rms(cv, conv_g, CONV_HEADS)], axis=-1) @ w_out

def hier_moe(h, w_group, w_router, w_gate, w_up, w_down):
    d = h.shape[-1]
    ht = h.reshape(-1, d)
    n = ht.shape[0]
    g_prob = jax.nn.softmax((ht @ w_group).astype(jnp.float32), axis=-1)
    g_sel = jnp.argmax(g_prob, axis=-1)
    g_w = jnp.take_along_axis(g_prob, g_sel[:, None], axis=1)[:, 0]
    e_logits = (ht @ w_router).astype(jnp.float32).reshape(n, N_GROUPS, EXPERTS_PER_GROUP)
    e_logits = jnp.take_along_axis(e_logits, g_sel[:, None, None], axis=1)[:, 0]
    e_prob = jax.nn.softmax(e_logits, axis=-1)
    top_p, top_i = lax.top_k(e_prob, TOP_K)
    top_p = top_p / jnp.sum(top_p, axis=-1, keepdims=True)
    wts = (g_w[:, None] * top_p).reshape(-1)
    eid = (g_sel[:, None] * EXPERTS_PER_GROUP + top_i).reshape(-1).astype(jnp.int32)
    tok = jnp.repeat(jnp.arange(n, dtype=jnp.int32), TOP_K)
    m = eid.shape[0]
    order = jnp.argsort(eid)
    s_e, s_tok, s_w = eid[order], tok[order], wts[order]
    counts = jnp.bincount(eid, length=N_EXPERTS).astype(jnp.int32)
    starts = jnp.cumsum(counts) - counts
    padded = ((counts + MOE_BLOCK - 1) // MOE_BLOCK) * MOE_BLOCK
    pstarts = jnp.cumsum(padded) - padded
    pends = pstarts + padded
    dest = pstarts[s_e] + (jnp.arange(m, dtype=jnp.int32) - starts[s_e])
    p_rows = m + N_EXPERTS * MOE_BLOCK
    n_blk = p_rows // MOE_BLOCK
    xbuf = jnp.zeros((p_rows, d), h.dtype).at[dest].set(ht[s_tok])
    blk_start = jnp.arange(n_blk, dtype=jnp.int32) * MOE_BLOCK
    blk_e = jnp.minimum(jnp.searchsorted(pends, blk_start, side='right'), N_EXPERTS - 1)

    def expert_block(args):
        xb, e = args
        return (jax.nn.silu(xb @ w_gate[e]) * (xb @ w_up[e])) @ w_down[e]

    ybuf = lax.map(expert_block, (xbuf.reshape(n_blk, MOE_BLOCK, d), blk_e)).reshape(p_rows, d)
    y = ybuf[dest] * s_w[:, None].astype(h.dtype)
    return jax.ops.segment_sum(y, s_tok, num_segments=n).reshape(h.shape)

def trunk_layer(x, ctx, c, c_ctx, cos, sin, w_mod, b_mod, norm1_g, w_in, q_norm_g, k_norm_g,
                conv_w, attn_out_g, conv_out_g, w_out, norm2_g, w_group, w_router, w_gate, w_up,
                w_down, update_ctx):
    sh1, sc1, gt1, sh2, sc2, gt2 = modulation(c, w_mod, b_mod)
    csh1, csc1, cgt1, csh2, csc2, cgt2 = modulation(c_ctx, w_mod, b_mod)
    hx = rms_norm(x, norm1_g) * (1.0 + sc1) + sh1
    hc = rms_norm(ctx, norm1_g) * (1.0 + csc1) + csh1
    qx, kx, vx, bx, cx, ux = in_proj(hx, w_in, q_norm_g, k_norm_g)
    qc, kc, vc, bc, cc, uc = in_proj(hc, w_in, q_norm_g, k_norm_g)
    qx = apply_axial_rope(qx, cos, sin)
    kx = apply_axial_rope(kx, cos, sin)
    k_all = jnp.concatenate([kc, kx], axis=1)
    v_all = jnp.concatenate([vc, vx], axis=1)
    ax = latent_attention(qx, k_all, v_all)
    convx = short_conv(bx, cx, ux, conv_w)
    x_new = x + gt1 * merge_out(ax, convx, attn_out_g, conv_out_g, w_out)
    hx2 = rms_norm(x_new, norm2_g) * (1.0 + sc2) + sh2
    x_new = x_new + gt2 * hier_moe(hx2, w_group, w_router, w_gate, w_up, w_down)
    if update_ctx:
        b = ctx.shape[0]
        ac = attend(qc.reshape(b, -1, N_KV_HEADS, KV_REP, HEAD_DIM), kc, vc).reshape(b, -1, ATTN_WIDTH)
        convc = short_conv(bc, cc, uc, conv_w)
        ctx = ctx + cgt1 * merge_out(ac, convc, attn_out_g, conv_out_g, w_out)
        hc2 = rms_norm(ctx, norm2_g) * (1.0 + csc2) + csh2
        ctx = ctx + cgt2 * hier_moe(hc2, w_group, w_router, w_gate, w_up, w_down)
    return x_new, ctx

def first_inputs(seed: int = 0) -> dict:
    key = jax.random.key(seed)
    ks = jax.random.split(key, 21)
    f32 = jnp.float32
    L, D = DEPTH, D_MODEL

    def nrm(k, shape, scale):
        return jax.random.normal(k, shape, f32) * scale

    return {
        "x": nrm(ks[0], (BATCH, SEQ, D), 1.0),
        "c": nrm(ks[1], (BATCH, D), 1.0),
        "ctx": nrm(ks[2], (BATCH, CTX_LEN, D), 1.0),
        "c_ctx": nrm(ks[3], (D,), 1.0),
        "w_mod": nrm(ks[4], (L, D, N_MOD * D), 0.5 * D ** -0.5),
        "b_mod": nrm(ks[5], (L, N_MOD * D), 0.02),
        "norm1_g": 1.0 + nrm(ks[6], (L, D), 0.02),
        "w_in": nrm(ks[7], (L, D, IN_COLS), D ** -0.5),
        "q_norm_g": 1.0 + nrm(ks[8], (L, HEAD_DIM), 0.02),
        "k_norm_g": 1.0 + nrm(ks[9], (L, HEAD_DIM), 0.02),
        "conv_w": nrm(ks[10], (L, CONV_K, CONV_WIDTH), CONV_K ** -0.5),
        "attn_out_g": 1.0 + nrm(ks[11], (L, ATTN_WIDTH), 0.02),
        "conv_out_g": 1.0 + nrm(ks[12], (L, CONV_WIDTH), 0.02),
        "w_out": nrm(ks[13], (L, MIX_WIDTH, D), MIX_WIDTH ** -0.5),
        "norm2_g": 1.0 + nrm(ks[14], (L, D), 0.02),
        "w_group": nrm(ks[15], (L, D, N_GROUPS), D ** -0.5),
        "w_router": nrm(ks[16], (L, D, N_EXPERTS), D ** -0.5),
        "w_gate": nrm(ks[17], (L, N_EXPERTS, D, D_EXPERT), D ** -0.5),
        "w_up": nrm(ks[18], (L, N_EXPERTS, D, D_EXPERT), D ** -0.5),
        "w_down": nrm(ks[19], (L, N_EXPERTS, D_EXPERT, D), D_EXPERT ** -0.5),
        "final_g": 1.0 + nrm(ks[20], (D,), 0.02),
    }

def first_block(x, c, ctx, c_ctx, w_mod, b_mod, norm1_g, w_in, q_norm_g, k_norm_g, conv_w,
              attn_out_g, conv_out_g, w_out, norm2_g, w_group, w_router, w_gate, w_up, w_down,
              final_g):
    cos, sin = axial_rope_tables(x.shape[1], x.dtype)
    for i in range(DEPTH):
        x, ctx = trunk_layer(x, ctx, c, c_ctx, cos, sin, w_mod[i], b_mod[i], norm1_g[i], w_in[i],
                             q_norm_g[i], k_norm_g[i], conv_w[i], attn_out_g[i], conv_out_g[i],
                             w_out[i], norm2_g[i], w_group[i], w_router[i], w_gate[i], w_up[i],
                             w_down[i], update_ctx=(i < DEPTH - 1))
    return rms_norm(x, final_g)


N_META = 16
CHUNK = 128
PAD = CHUNK - N_META
RET_HEADS = 4
RET_DK = D_MODEL // RET_HEADS
RET_DV = 2 * RET_DK
SB_HEADS = D_MODEL // 64
SB_DH = 64
D_FF = -(-8 * D_MODEL // (3 * 256)) * 256
ROPE_BASE = 10000.0
NORM_EPS = 1e-6
GN_EPS = 1e-5
PROJ_SPLIT = (
    RET_HEADS * RET_DK,
    RET_HEADS * RET_DK,
    RET_HEADS * RET_DV,
    RET_HEADS * RET_DV,
    SB_HEADS * SB_DH,
    SB_HEADS * SB_DH,
    SB_HEADS * SB_DH,
    D_MODEL,
    D_MODEL,
)
PROJ_WIDTH = sum(PROJ_SPLIT)


def rmsnorm(x, g):
    xf = x.astype(jnp.float32)
    y = xf * lax.rsqrt(jnp.mean(xf * xf, axis=-1, keepdims=True) + NORM_EPS)
    return (y * g.astype(jnp.float32)).astype(x.dtype)

def rotary(x, pos):
    half = x.shape[-1] // 2
    inv = ROPE_BASE ** (-jnp.arange(half, dtype=jnp.float32) / half)
    ang = pos[:, None] * inv[None, :]
    cos, sin = jnp.cos(ang), jnp.sin(ang)
    x1, x2 = x[..., :half], x[..., half:]
    return jnp.concatenate([x1 * cos - x2 * sin, x1 * sin + x2 * cos], axis=-1)

def retention_chunkwise(q, k, v):
    B, H, Lp, dk = q.shape
    dv = v.shape[-1]
    n = Lp // CHUNK
    log_g = jnp.log1p(-(2.0 ** (-5.0 - jnp.arange(H, dtype=jnp.float32))))
    idx = jnp.arange(CHUNK, dtype=jnp.float32)
    diff = idx[:, None] - idx[None, :]
    decay = jnp.where(diff >= 0, jnp.exp(log_g[:, None, None] * jnp.maximum(diff, 0.0)), 0.0)
    zeta = jnp.exp(log_g[:, None] * (CHUNK - 1.0 - idx))[:, :, None]
    xi = jnp.exp(log_g[:, None] * (idx + 1.0))[:, :, None]
    g_chunk = jnp.exp(log_g * CHUNK)[:, None, None]

    qc = q.reshape(B, H, n, CHUNK, dk)
    kc = k.reshape(B, H, n, CHUNK, dk)
    vc = v.reshape(B, H, n, CHUNK, dv)
    scores = jnp.einsum('bhncd,bhnsd->bhncs', qc, kc) * decay[:, None]
    inner = jnp.einsum('bhncs,bhnse->bhnce', scores, vc)

    def step(state, inp):
        q_i, k_i, v_i = inp
        cross = jnp.einsum('bhcd,bhde->bhce', q_i, state) * xi
        state = g_chunk * state + jnp.einsum('bhsd,bhse->bhde', k_i, v_i * zeta)
        return state, cross

    s0 = jnp.zeros((B, H, dk, dv), jnp.float32)
    _, cross = lax.scan(step, s0, (qc.transpose(2, 0, 1, 3, 4), kc.transpose(2, 0, 1, 3, 4), vc.transpose(2, 0, 1, 3, 4)))
    out = inner + cross.transpose(1, 2, 0, 3, 4)
    return out.reshape(B, H, Lp, dv)

def head_groupnorm(y):
    mu = jnp.mean(y, axis=-1, keepdims=True)
    var = jnp.mean(jnp.square(y - mu), axis=-1, keepdims=True)
    return (y - mu) * lax.rsqrt(var + GN_EPS)

def stick_breaking(q, k, v):
    Lp, d = q.shape[2], q.shape[3]
    scale = d ** -0.5
    outs = []
    for i in range(Lp // CHUNK):
        lk = (i + 1) * CHUNK
        q_blk = q[:, :, i * CHUNK:lk]
        k_pre, v_pre = k[:, :, :lk], v[:, :, :lk]
        z = jnp.einsum('bhtd,bhsd->bhts', q_blk, k_pre) * scale
        t_pos = i * CHUNK + jnp.arange(CHUNK)
        s_pos = jnp.arange(lk)
        valid = (s_pos[None, :] < t_pos[:, None]) & (s_pos[None, :] >= PAD)
        log_not = jnp.where(valid, jax.nn.log_sigmoid(-z), 0.0)
        after = lax.cumsum(log_not, axis=3, reverse=True) - log_not
        a = jnp.where(valid, jnp.exp(jax.nn.log_sigmoid(z) + after), 0.0)
        outs.append(jnp.einsum('bhts,bhse->bhte', a, v_pre))
    return jnp.concatenate(outs, axis=2)

def hybrid_mixer(hn, w_in, w_ret_out, w_sb_out, w_out):
    B, L, _ = hn.shape
    dtype = hn.dtype
    proj = hn @ w_in
    rq, rk, rv, rg, sq, sk, sv, ga, gb = jnp.split(proj, list(np.cumsum(PROJ_SPLIT)[:-1]), axis=-1)

    def heads(t, h):
        t = t.reshape(B, L, h, -1).transpose(0, 2, 1, 3).astype(jnp.float32)
        return jnp.pad(t, ((0, 0), (0, 0), (PAD, 0), (0, 0)))

    def merge_heads(t):
        t = t[:, :, PAD:]
        return t.transpose(0, 2, 1, 3).reshape(B, L, -1)

    pos = jnp.arange(L + PAD, dtype=jnp.float32) - PAD
    q_r = rotary(heads(rq, RET_HEADS), pos) * (RET_DK ** -0.5)
    k_r = rotary(heads(rk, RET_HEADS), pos)
    y_ret = head_groupnorm(retention_chunkwise(q_r, k_r, heads(rv, RET_HEADS)))
    y_ret = (jax.nn.silu(rg.astype(jnp.float32)) * merge_heads(y_ret)).astype(dtype) @ w_ret_out
    y_sb = merge_heads(stick_breaking(heads(sq, SB_HEADS), heads(sk, SB_HEADS), heads(sv, SB_HEADS)))
    y_sb = y_sb.astype(dtype) @ w_sb_out
    merged = jax.nn.sigmoid(ga) * y_ret + jax.nn.sigmoid(gb) * y_sb
    return merged @ w_out

def swiglu(hn, w_ffn_in, w_ffn_out):
    a, b = jnp.split(hn @ w_ffn_in, 2, axis=-1)
    return (jax.nn.silu(a) * b) @ w_ffn_out

def second_inputs(seed: int = 0) -> dict:
    key = jax.random.key(seed)
    ks = jax.random.split(key, 12)
    f32 = jnp.float32
    nrm = lambda k, shape, fan: jax.random.normal(k, shape, f32) * (fan ** -0.5)
    gain = lambda k: 1.0 + 0.02 * jax.random.normal(k, (DEPTH, D_MODEL), f32)
    return {
        "x": jax.random.normal(ks[0], (BATCH, SEQ, D_MODEL), f32),
        "meta_tokens": jax.random.normal(ks[1], (N_META, D_MODEL), f32),
        "w_in": nrm(ks[2], (DEPTH, D_MODEL, PROJ_WIDTH), D_MODEL),
        "w_ret_out": nrm(ks[3], (DEPTH, RET_HEADS * RET_DV, D_MODEL), RET_HEADS * RET_DV),
        "w_sb_out": nrm(ks[4], (DEPTH, SB_HEADS * SB_DH, D_MODEL), SB_HEADS * SB_DH),
        "w_out": nrm(ks[5], (DEPTH, D_MODEL, D_MODEL), D_MODEL),
        "w_ffn_in": nrm(ks[6], (DEPTH, D_MODEL, 2 * D_FF), D_MODEL),
        "w_ffn_out": nrm(ks[7], (DEPTH, D_FF, D_MODEL), D_FF),
        "norm_mix_pre": gain(ks[8]),
        "norm_mix_post": gain(ks[9]),
        "norm_ffn_pre": gain(ks[10]),
        "norm_ffn_post": gain(ks[11]),
    }

def second_block(x, meta_tokens, w_in, w_ret_out, w_sb_out, w_out, w_ffn_in, w_ffn_out,
              norm_mix_pre, norm_mix_post, norm_ffn_pre, norm_ffn_post):
    B = x.shape[0]
    meta = jnp.broadcast_to(meta_tokens.astype(x.dtype)[None], (B, N_META, x.shape[-1]))
    h = jnp.concatenate([meta, x], axis=1)
    for l in range(DEPTH):
        mix = hybrid_mixer(rmsnorm(h, norm_mix_pre[l]), w_in[l], w_ret_out[l], w_sb_out[l], w_out[l])
        h = h + rmsnorm(mix, norm_mix_post[l])
        ff = swiglu(rmsnorm(h, norm_ffn_pre[l]), w_ffn_in[l], w_ffn_out[l])
        h = h + rmsnorm(ff, norm_ffn_post[l])
    return h[:, N_META:]


def setup_inputs(seed=0):
    out = dict(first_inputs(seed))
    for name, value in second_inputs(seed + 1).items():
        if name != "x":
            out[name + "_2"] = value
    return out


def reference(
    x, c, ctx, c_ctx, w_mod, b_mod, norm1_g, w_in, q_norm_g, k_norm_g, conv_w, attn_out_g,
    conv_out_g, w_out, norm2_g, w_group, w_router, w_gate, w_up, w_down, final_g, meta_tokens_2,
    w_in_2, w_ret_out_2, w_sb_out_2, w_out_2, w_ffn_in_2, w_ffn_out_2, norm_mix_pre_2,
    norm_mix_post_2, norm_ffn_pre_2, norm_ffn_post_2,
):
    x = first_block(
        x, c, ctx, c_ctx, w_mod, b_mod, norm1_g, w_in, q_norm_g, k_norm_g, conv_w, attn_out_g,
        conv_out_g, w_out, norm2_g, w_group, w_router, w_gate, w_up, w_down, final_g,
    )
    return second_block(
        x, meta_tokens_2, w_in_2, w_ret_out_2, w_sb_out_2, w_out_2, w_ffn_in_2, w_ffn_out_2,
        norm_mix_pre_2, norm_mix_post_2, norm_ffn_pre_2, norm_ffn_post_2,
    )


_drawn_inputs = setup_inputs


def setup_inputs(seed=0):
    import zlib

    import numpy as np

    out = dict(_drawn_inputs(seed))
    spreads = {}
    factors = {'norm1_g': 3.33,
     'q_norm_g': 8.0,
     'k_norm_g': 6.264,
     'attn_out_g': 4.248,
     'conv_out_g': 7.474,
     'norm2_g': 3.214,
     'norm_mix_post_2': 3.342,
     'norm_ffn_pre_2': 3.456,
     'norm_ffn_post_2': 4.617}
    for name, (base, spread) in spreads.items():
        noise = np.random.default_rng([zlib.crc32(name.encode()), seed]).standard_normal(out[name].shape)
        drawn = base * np.exp(spread * noise) if base else spread * noise
        out[name] = __import__('jax').numpy.asarray(drawn.astype(out[name].dtype))
    for name, factor in factors.items():
        out[name] = (out[name] * factor).astype(out[name].dtype)
    return out
```

```python
from contextlib import ExitStack

import concourse.bass as bass
import numpy as np
from concourse import mybir

F32 = mybir.dt.float32
I32 = mybir.dt.int32
U32 = mybir.dt.uint32
ALU = mybir.AluOpType
ACT = mybir.ActivationFunctionType
AX = mybir.AxisListType.X

P = 128
D = 1024
KD = D // P
TOK = 256
TT = TOK // P
HEADS, HD, KVH = 8, 64, 2
CV = 4
E, EG, FE = 32, 4, 768
JE = FE // P
CAP = 32
SWEEPS = TOK // CAP
EPS, GN_EPS = 1e-6, 1e-5
BIG = 1e30
SLOT = KD * FE
PAIRS = E // 2

META = 16
LK = META + TOK
RH, RDV, RDK = 4, 512, 256
SH = 16
FF = 2816
FB = FF // P
CW = 512
CSLOT = KD * CW
CSLOTS = 4
DIAG = 3 * P

CA = dict(ident=(0, P), ones=(128, P), before=(256, P), headmean=(384, P), iota=(512, E), iota4p8=(544, EG),
          iota4=(548, EG), steps7=(552, 7), rope_cos=(568, 64), rope_sin=(632, 64))
CA_N = 696
CC = dict(cos=(0, LK), sin=(LK, LK), negtri=(544, P), negones=(672, P), valid=(800, P), invalid=(928, DIAG),
          decay=(1312, RH * DIAG), decay_meta=(1312 + RH * DIAG, RH * TOK))
CC_N = 1312 + RH * DIAG + RH * TOK

VEC = dict(norm1_g=(0, 8), attn_out_g=(8, 4), conv_out_g=(12, 4), conv_w=(16, 12), norm_mix_pre_2=(28, 8),
           norm_ffn_pre_2=(36, 8))
VEC_N = 44

QKV_JOBS = [(0, False), (1, False), (2, True), (2, False), (3, True), (3, False)]
SB_ORDER = [0, 2, 4, 6, 1, 3, 5, 7, 8, 10, 12, 14, 9, 11, 13, 15]
SB_BANKS = [0, 1, 2, 7]


def build(nc, A, out):
    ctx = ExitStack()
    with ctx:
        def sem(name):
            return ctx.enter_context(nc.semaphore(name))

        mem = ctx.enter_context(nc.sbuf_tensor("mem", [P, 52900], F32))
        PS = ctx.enter_context(nc.psum_tensor("PS", [P, 8, 512], F32))
        top_idx = ctx.enter_context(nc.sbuf_tensor("top_idx", [P, TT, 8], U32))
        row_ids = ctx.enter_context(nc.sbuf_tensor("row_ids", [P, TT, 2], I32))
        extra_i = ctx.enter_context(nc.sbuf_tensor("extra_i", [P, 1], I32))

        mod_d = nc.dram_tensor("mod_rows", [2, 6 * D], F32, kind="Internal").ap()
        ybuf = nc.dram_tensor("expert_rows", [E * CAP, D], F32, kind="Internal").ap()

        class Region:

            def __init__(self, base, size):
                self.at, self.end = base, base + size

            def take(self, *dims):
                n = 1
                for d in dims:
                    n *= d
                o = self.at
                self.at += n
                assert self.at <= self.end, (self.at, self.end)
                return shaped(mem[:, o:o + n], *dims)

        def shaped(ap, *dims):
            if len(dims) == 2:
                return ap.rearrange("p (a b) -> p a b", a=dims[0])
            if len(dims) == 3:
                return ap.rearrange("p (a b c) -> p a b c", a=dims[0], b=dims[1])
            return ap

        def flat(ap):
            return ap.rearrange("p a b -> p (a b)")

        slots = mem[:, 0:6 * SLOT].rearrange("p (s n) -> p s n", s=6)
        keep = Region(6 * SLOT, 52900 - 6 * SLOT)
        consts = keep.take(CA_N)
        K = {n: consts[:, o:o + w] for n, (o, w) in CA.items()}
        ident = K["ident"]
        xrow = keep.take(TT, D)
        vecT = keep.take(VEC_N)
        V = {n: vecT[:, o:o + w] for n, (o, w) in VEC.items()}
        small = keep.take(704)
        at_h2 = keep.at
        h2row = keep.take(TT, D)
        gate2 = keep.take(D)
        at_rows = keep.at
        scale2, shift2, gate1 = keep.take(D), keep.take(D), keep.take(D)
        mixT = keep.take(KD, TOK)
        at_bias = keep.at
        bias = keep.take(8, 192)
        condT = keep.take(KD, 32)
        w_route = keep.take(KD, EG + E)
        xTe = keep.take(2, KD, CAP)
        hTe = keep.take(2, JE, CAP)
        silu_g, hmid = keep.take(192), keep.take(192)
        yexp = keep.take(2, 256)
        pick = keep.take(2, TT, CAP)
        posadj = keep.take(TT, E)
        iota_r = keep.take(CAP)

        sm = Region(6 * SLOT + CA_N + TT * D + VEC_N, 704)
        sumsq, rstd = sm.take(16), sm.take(16)
        negmax, psums, precip, mx = sm.take(16), sm.take(16), sm.take(16), sm.take(16)
        hss, hrs = sm.take(20), sm.take(20)
        mhalf, eps_col, gneps = sm.take(1), sm.take(1), sm.take(1)
        bn, mv = sm.take(TT, 6), sm.take(TT, 2)
        logits = sm.take(TT, EG + E)
        gmax, gsum, ed, den = sm.take(TT), sm.take(TT), sm.take(TT), sm.take(TT)
        gexp, gsel = sm.take(TT, EG), sm.take(TT)
        goh, gcand = sm.take(TT, EG), sm.take(TT, EG)
        emask = sm.take(TT, E)
        top8 = sm.take(TT, 8)
        top_e, rank_e, wts = sm.take(TT, 2), sm.take(TT, 2), sm.take(TT, 2)
        steps_hit = sm.take(TT * 2, 7)
        ids_f, sweep_e, wts_now, sweep_now = sm.take(TT, 2), sm.take(TT, 2), sm.take(TT, 2), sm.take(1)
        maxc, hit7, extra_f = sm.take(1), sm.take(7), sm.take(1)

        scr = Region(3 * SLOT, 3 * SLOT)
        hT = scr.take(KD, 512)
        ctxrow = scr.take(TT, D)
        gbT, gcT = shaped(ctxrow[:, 0, :], CV, TOK), shaped(ctxrow[:, 1, :], CV, TOK)
        qk = scr.take(4, 640)
        vrow = scr.take(4, P)
        qT = scr.take(4, TOK)
        kT = scr.take(512)
        xn = shaped(mem[:, scr.at:scr.at + 2 * D], 2, D)
        probs = scr.take(2, 512)
        pT = scr.take(2, 4, P)
        arow = scr.take(TT, 512)
        vTc = scr.take(CV, TOK + 2)
        yT = scr.take(CV, TOK)
        sqT = scr.take(CV, TOK)
        modrow = scr.take(5, 192)
        h2T = hT[:, :, 0:TOK]
        onehot = mem[:, scr.at:scr.at + 128].rearrange("p (t k e) -> p t k e", t=TT, k=2)
        scr.take(128)
        chosen, rank, oh_rank = shaped(flat(qk)[:, 0:64], TT, E), shaped(flat(qk)[:, 64:128], TT, E), \
            flat(qk)[:, 128:256].rearrange("p (t k e) -> p t k e", t=TT, k=2)
        counts = flat(qk)[:, 256:288]
        vec, vec2 = flat(sqT)[0:VEC_N, 0:P], flat(sqT)[0:32, P:2 * P]
        rope_tmp = flat(sqT)[:, 256:1024]
        crow = shaped(flat(yT)[:, 0:16], 2, KD)
        mods = shaped(flat(yT)[:, 16:48], 2, 16)
        headg = flat(yT)[:, 48:176]
        qk_sq = flat(modrow)[:, 0:640]

        cslots = mem[:, 0:CSLOTS * CSLOT].rearrange("p (s n) -> p s n", s=CSLOTS)
        tail = Region(CSLOTS * CSLOT, 6 * SLOT - CSLOTS * CSLOT)
        shared = tail.take(FB * TOK)
        final_g = shared[:, 0:D]
        ygat = [[scale2, shift2], [gate1, flat(bias)[:, 0:D]]]
        moe = flat(mixT).rearrange("p (t d) -> p t d", t=TT)
        yrT = shaped(shared[:, 0:16 * TOK], 16, TOK)
        gT = shaped(shared, FB, TOK)
        qR, kR = tail.take(KD, TOK), tail.take(KD, LK)
        merged = qR
        vbuf = tail.take(2, TT, RDV)
        vmbuf = tail.take(2, RDV)
        vS, vmS = shaped(vbuf.rearrange("p a b c -> p (a b c)"), TT, D), flat(vmbuf)
        yr = tail.take(2, TT, RDV)
        metarow = yr.rearrange("p a b c -> p (a b c)")[0:META, 0:D]
        ysbT = shaped(yr.rearrange("p a b c -> p (a b c)"), KD, TOK)
        hnrow = tail.take(2, D)
        gsig = flat(hnrow)
        rot_tmp = flat(hnrow)[:, 0:4 * LK]
        gn_tmp = flat(hnrow)[:, 0:TT * RDV]
        at_s = tail.at
        sT = tail.take(RH, DIAG)
        sTm = tail.take(RH, TOK)
        sbr = Region(at_s, 6 * SLOT - at_s)
        EL, aT = sbr.take(3, DIAG), sbr.take(6, DIAG)
        hnT = shaped(mem[:, at_h2:at_h2 + KD * LK], KD, LK)
        rest = Region(at_h2 + KD * LK, at_rows - at_h2 - KD * LK)
        Lm, aTm = rest.take(TOK), rest.take(2, TOK)
        late = Region(at_rows, 3 * D + KD * TOK)
        consts2 = late.take(CC_N)
        K2 = {n: consts2[:, o:o + w] for n, (o, w) in CC.items()}
        mixpost = late.take(D)
        lateb = Region(at_bias, 1536 + 256 + 288)
        ffnpost = lateb.take(D)
        ff_tmp = lateb.take(2, 2 * TOK)

        S = {}
        for n in ("ld_consts ld_x ld_ctx ld_c ld_vec ld_bias ld_headg ld_route ld_norm2 set_bias set_cond cond_ready "
                  "sq_done rstd_done xn_ready xnT_psum xnT_evac vec_psum vec_ready mod_psum modA_rows modA_out "
                  "ld_vec2 vec2_psum mod_ready hT_ready qkv_psum qkv_evac gbgc_psum gbgc_evac u_psum u_evac "
                  "modB_rows modB_out ld_rowmods qksq_done qksq_sum qk_rstd qk_ready qkT_psum qkT_ready "
                  "conv_ready convsq_done convms_psum convsd_done conv_done s_psum negmax_ready p_ready pT_psum pT_ready pv_psum "
                  "a_sum a_rstd a_ready aT_psum mixT_ready xo_psum x_new xsq_done x_rstd h2_ready h2T_psum h2T_ready "
                  "logit_psum gexp_in gexp_out eexp_in eexp_out onehot_ready rank_psum route_ready "
                  "pick_ready xe_psum xe_ready gu_psum silu_ready he_ready ye_psum "
                  "moe_out gather_starts ld_final yg_loaded x1_pre fsq_done f_rstd x1_ready ld_consts2 ld_meta ld_posts ld_norm "
                  "nsq_done n_rstd hn_ready hnT_psum hnT_ready rqk_psum rot_done rs_psum rs_ready v_psum v_evac rg_psum rg_silu "
                  "y_psum y_var y_rstd yr_ready yrT_psum yrT_evac sqk_psum sqk_evac sv_psum sv_evac vm_copied "
                  "mz_psum splm_done Lm_ready z_psum spl_done L_ready cum_psum arg_done aT_ready aTm_ready head_done ysb_evac "
                  "ro_psum so_psum quad_psum quad_sig merge_done mix_psum mixsq_done mix_rstd h_ready ff_psum ff_silu ff_ready "
                  "fo_psum fosq_done fo_rstd out_ready out_done").split():
            S[n] = sem(n)
        w_full = [sem(f"w_full{i}") for i in range(6)]
        y_out = [sem(f"y_out{i}") for i in range(2)]
        c_full = [sem(f"c_full{i}") for i in range(CSLOTS)]

        w_mod = A["w_mod"].rearrange("(p c) n -> p c n", c=KD)
        w_in = A["w_in"].rearrange("(c p) n -> p c n", p=P)
        w_out = A["w_out"].rearrange("(c p) n -> p c n", p=P)
        firsts = ([(w_mod, n, FE, "mod_psum", n + 1) for n in range(3)]
                  + [(w_in, 0, FE, "qkv_psum", 6), (w_in, 1, FE, "gbgc_psum", 6), (w_in, 2, FE, "u_psum", CV)]
                  + [(w_mod, n, FE, "mod_psum", n + 1) for n in range(3, 8)]
                  + [(w_out, n, CW, "xo_psum", 2 * n + 2) for n in range(2)])
        WIN, MODB, WOUT = 3, 6, 11
        used = [len([n for n in range(len(firsts)) if n % 3 == s]) for s in range(3)] + [0, 0, 0]
        w_gate = A["w_gate"].rearrange("e (p c) f -> p e c f", c=KD)
        w_up = A["w_up"].rearrange("e (p c) f -> p e c f", c=KD)
        w_down = A["w_down"].rearrange("e (p j) d -> p e j d", j=JE)

        def chunk(n):
            w = firsts[n][2]
            return shaped(slots[:, n % 3, 0:KD * w], KD, w)

        def chunk_landed(eng, n):
            eng.wait_ge(w_full[n % 3], 16 * (n // 3 + 1))

        w2 = A["w_in_2"].rearrange("(c p) n -> p c n", p=P)
        w_ro = A["w_ret_out_2"].rearrange("(c p) n -> p c n", p=P)
        w_so = A["w_sb_out_2"].rearrange("(c p) n -> p c n", p=P)
        w_o2 = A["w_out_2"].rearrange("(c p) n -> p c n", p=P)
        w_fi = A["w_ffn_in_2"].rearrange("(c p) (u n) -> p c u n", p=P, u=2)
        w_fo = A["w_ffn_out_2"].rearrange("(c p) n -> p c n", p=P)
        seconds = []
        C2 = {}

        def stream(name, i, src, dims, done, value):
            C2[name, i] = len(seconds)
            seconds.append((src, dims, done, value))

        def cols(w, i, n=CW):
            return w[:, :, i * n:(i + 1) * n]

        wide_chunk = (KD, CW)
        for i in range(2):
            stream("rq", i, cols(w2, i), wide_chunk, "rqk_psum", 2 * i + 2)
        for i in range(2):
            stream("rk", i, cols(w2, 2 + i), wide_chunk, "rqk_psum", RH + 2 * i + 2)
        for h in range(RH):
            stream("rv", h, cols(w2, 4 + h), wide_chunk, "v_psum", h + 1)
            stream("rg", h, cols(w2, 8 + h), wide_chunk, "rg_psum", h + 1)
        for i in range(2):
            stream("sq", i, cols(w2, 12 + i), wide_chunk, "sqk_psum", 4 * i + 4)
        for i in range(2):
            stream("sk", i, cols(w2, 14 + i), wide_chunk, "sqk_psum", KD + 4 * i + 4)
        for i in range(2):
            stream("sv", i, cols(w2, 16 + i), wide_chunk, "sv_psum", i + 1)
        for i in range(2):
            for j in (2 * i, 2 * i + 1):
                stream("ro", j, cols(w_ro, j, 256), (16, 256), "ro_psum", j + 1)
            stream("ga", i, cols(w2, 18 + i), wide_chunk, "quad_psum", i + 1)
        for i in range(2):
            stream("so", i, cols(w_so, i), wide_chunk, "so_psum", i + 1)
            stream("gb", i, cols(w2, 20 + i), wide_chunk, "quad_psum", i + 3)
        for i in range(2):
            stream("o2", i, cols(w_o2, i), wide_chunk, "mix_psum", i + 1)
        for i in range(FB // 2):
            stream("fi", i, w_fi[:, :, :, i * 256:(i + 1) * 256], (KD, 2, 256), "ff_psum", i + 1)
        for i in range(0, FB, 4):
            stream("fo", i // 4, w_fo[:, i:min(i + 4, FB), :], (min(4, FB - i), D), "fo_psum", i // 4 + 1)

        def chunk2(name, i):
            n = C2[name, i]
            dims = seconds[n][1]
            size = 1
            for d in dims:
                size *= d
            return shaped(cslots[:, n % CSLOTS, 0:size], *dims)

        def chunk2_landed(eng, name, i):
            n = C2[name, i]
            before = [len(seconds[m][1]) == 3 for m in range(n % CSLOTS, n + 1, CSLOTS)]
            eng.wait_ge(c_full[n % CSLOTS], 16 * (len(before) + sum(before)))

        def evac_sb(a, G):
            r = 64 * (G % 2)
            a.wait_ge(S["head_done"], 4 * G + 4)
            a.activation(flat(ysbT[r:r + 64, 4 * (G // 2):4 * (G // 2) + 4, :]), flat(PS[r:r + 64, 5:7, :]), ACT.Copy)\
                .then_inc(S["ysb_evac"], 1)

        block = ctx.enter_context(nc.Block())

        @block.sync
        def _(sp):
            for n, (w, i, width, _, _) in enumerate(firsts):
                if n >= 3:
                    sp.wait_ge(S[firsts[n - 3][3]], firsts[n - 3][4])
                sp.dma_start(chunk(n), w[:, :, i * width:(i + 1) * width]).then_inc(w_full[n % 3], 16)

            def load(s, e):
                w = (w_gate, w_up, w_down)[s % 3]
                dst = slots[:, s, :].rearrange("p (o c f) -> p o c f", o=1, f=w.shape[-1])
                sp.dma_start(dst, w[:, bass.ds(e, 1)]).then_inc(w_full[s], 16)

            def load_pair(it, before):
                for h in range(2):
                    for s in range(3 * h, 3 * h + 3):
                        sp.wait_ge(S["gu_psum"] if s % 3 < 2 else S["ye_psum"], before * 2 + (h + 1))
                        load(s, it * 2 + h)

            for s in range(6):
                if s < 3:
                    last = max(n for n in range(len(firsts)) if n % 3 == s)
                    sp.wait_ge(S[firsts[last][3]], firsts[last][4])
                elif s == 3:
                    sp.wait_ge(S["route_ready"], 1)
                load(s, s // 3)
            with sp.Fori(0, PAIRS - 1) as it:
                load_pair(it + 1, it)
            extra = sp.value_load(extra_i[0:1, 0:1], min_val=0, max_val=SWEEPS - 1)
            with sp.If(extra > 0):
                with sp.Fori(0, extra) as r:
                    with sp.Fori(0, PAIRS) as it:
                        load_pair(it, r * PAIRS + it + (PAIRS - 1))

            sp.wait_ge(S["ye_psum"], extra * E + (E - 1))
            for n, (src, dims, _, _) in enumerate(seconds):
                if n >= CSLOTS:
                    sp.wait_ge(S[seconds[n - CSLOTS][2]], seconds[n - CSLOTS][3])
                size = 1
                for d in dims:
                    size *= d
                dst = shaped(cslots[:, n % CSLOTS, 0:size], *dims)
                parts = [(dst[:, :, u], src[:, :, u]) for u in range(2)] if len(dims) == 3 else [(dst, src)]
                for to, of in parts:
                    sp.dma_start(to, of).then_inc(c_full[n % CSLOTS], 16)

        @block.gpsimd
        def _(g):
            g.memset(flat(bias), 0.0).then_inc(S["set_bias"], 1)
            g.memset(flat(condT), 0.0).then_inc(S["set_cond"], 1)
            g.memset(mhalf, -0.5)
            g.memset(eps_col, EPS)
            g.drain()
            g.wait_ge(S["set_bias"], 1)
            b_src = A["b_mod"].rearrange("o (n g q) -> o g n q", g=4, q=192)
            for gg in range(4):
                for r in range(2):
                    g.dma_start(bias[32 * gg + r:32 * gg + r + 1], b_src[:, gg]).then_inc(S["ld_bias"], 16)

            def power(dst, src, n, scale, eps=EPS):
                g.tensor_scalar(dst, src, scale, eps, ALU.mult, ALU.add)
                g.drain()
                return g.tensor_tensor(dst, dst, mhalf.to_broadcast([P, n]), ALU.pow)

            for i in range(4):
                g.wait_ge(S["sq_done"], i + 1)
                power(rstd[:, i:i + 1], sumsq[:, i:i + 1], 1, 1.0 / D).then_inc(S["rstd_done"], 1)

            def store_mod(n0, n1, done):
                rows = mod_d[:, n0 * FE:n1 * FE].rearrange("r (n g q) -> r g n q", g=4, q=192)
                for gg in range(4):
                    g.dma_start(rows[:, gg], modrow[32 * gg:32 * gg + 2, 0:n1 - n0, :]).then_inc(done, 16)
                g.wait_ge(done, 64)

            g.wait_ge(S["modA_rows"], 1)
            store_mod(0, 3, S["modA_out"])
            for r in range(2):
                g.dma_start(vec2[16 * r:16 * r + 16, :],
                            mod_d[r, 0:2 * D].rearrange("(a p) -> a p", p=P)).then_inc(S["ld_vec2"], 16)

            for t in range(4):
                g.wait_ge(S["qksq_sum"], t + 1)
                n = 2 if t < 2 else 10
                power(hrs[:, 0:n], hss[:, 0:n], n, 1.0 / HD).then_inc(S["qk_rstd"], 1)

            g.wait_ge(S["modB_rows"], 1)
            store_mod(3, 8, S["modB_out"])
            for dst, i in ((gate1, 2), (shift2, 3), (scale2, 4), (gate2, 5)):
                g.dma_start(dst, mod_d[0:1, i * D:(i + 1) * D].to_broadcast([P, D])).then_inc(S["ld_rowmods"], 16)

            for t in range(TT):
                g.wait_ge(S["a_sum"], t + 1)
                power(hrs[:, 0:8], hss[:, 0:8], 8, 1.0 / HD).then_inc(S["a_rstd"], 1)
            for t in range(TT):
                g.wait_ge(S["xsq_done"], t + 1)
                power(rstd[:, 4 + t:5 + t], sumsq[:, 4 + t:5 + t], 1, 1.0 / D).then_inc(S["x_rstd"], 1)

            def gather():
                for t in range(TT):
                    for k in range(2):
                        g.indirect_dma_start(ygat[t][k], None, ybuf,
                                             bass.IndirectOffsetOnAxis(row_ids[:, t, k:k + 1], 0)).then_inc(S["yg_loaded"], 16)

            g.wait_ge(S["moe_out"], 1)
            gather()
            extra = g.value_load(extra_i[0:1, 0:1], min_val=0, max_val=SWEEPS - 1)
            with g.If(extra > 0):
                with g.Fori(0, extra) as r:
                    g.wait_ge(S["moe_out"], r + 2)
                    g.sem_inc(S["gather_starts"], 1)
                    gather()
            for t in range(TT):
                g.wait_ge(S["fsq_done"], t + 1)
                power(rstd[:, 6 + t:7 + t], sumsq[:, 6 + t:7 + t], 1, 1.0 / D).then_inc(S["f_rstd"], 1)

            for i in range(3):
                n = META if i == 0 else P
                g.wait_ge(S["nsq_done"], i + 1)
                g.tensor_scalar(rstd[0:n, 8 + i:9 + i], sumsq[0:n, 8 + i:9 + i], 1.0 / D, EPS, ALU.mult, ALU.add)
                g.drain()
                g.tensor_tensor(rstd[0:n, 8 + i:9 + i], rstd[0:n, 8 + i:9 + i], mhalf[0:n], ALU.pow).then_inc(S["n_rstd"], 1)
            for n in range(RH):
                g.wait_ge(S["y_var"], n + 1)
                g.tensor_scalar(mv[:, :, 1], mv[:, :, 1], 1.0, GN_EPS, ALU.mult, ALU.add)
                g.drain()
                g.tensor_tensor(mv[:, :, 1], mv[:, :, 1], mhalf.to_broadcast([P, TT]), ALU.pow).then_inc(S["y_rstd"], 1)
            for t in range(TT):
                g.wait_ge(S["mixsq_done"], t + 1)
                power(rstd[:, 11 + t:12 + t], sumsq[:, 11 + t:12 + t], 1, 1.0 / D).then_inc(S["mix_rstd"], 1)
            for t in range(TT):
                g.wait_ge(S["nsq_done"], 4 + t)
                power(rstd[:, 8 + t:9 + t], sumsq[:, 8 + t:9 + t], 1, 1.0 / D).then_inc(S["n_rstd"], 1)
            for t in range(TT):
                g.wait_ge(S["fosq_done"], t + 1)
                power(rstd[:, 13 + t:14 + t], sumsq[:, 13 + t:14 + t], 1, 1.0 / D).then_inc(S["fo_rstd"], 1)

        @block.scalar
        def _(a):
            a.dma_start(consts, A["consts_a"]).then_inc(S["ld_consts"], 16)
            a.dma_start(ctxrow, A["ctx"].rearrange("b (t p) d -> p (b t) d", p=P)).then_inc(S["ld_ctx"], 16)
            a.dma_start(xrow, A["x"].rearrange("b (t p) d -> p (b t) d", p=P)).then_inc(S["ld_x"], 16)
            a.dma_start(crow[:, 0, :], A["c"].rearrange("b (p c) -> p (b c)", c=KD)).then_inc(S["ld_c"], 16)
            a.dma_start(crow[:, 1, :], A["c_ctx"].rearrange("(p c) -> p c", c=KD)).then_inc(S["ld_c"], 16)
            for name, (o, n) in VEC.items():
                src = A[name]
                src = src.rearrange("k (a p) -> (k a) p", p=P) if name == "conv_w" else \
                    src.rearrange("o (a p) -> (o a) p", p=P)
                a.dma_start(vec[o:o + n, :], src).then_inc(S["ld_vec"], 16)
            a.dma_start(headg[:, 0:64], A["q_norm_g"].to_broadcast([P, HD])).then_inc(S["ld_headg"], 16)
            a.dma_start(headg[:, 64:128], A["k_norm_g"].to_broadcast([P, HD])).then_inc(S["ld_headg"], 16)
            a.dma_start(w_route[:, :, 0:EG], A["w_group"].rearrange("(c p) n -> p c n", p=P)).then_inc(S["ld_route"], 16)
            a.dma_start(w_route[:, :, EG:EG + E], A["w_router"].rearrange("(c p) n -> p c n", p=P)).then_inc(S["ld_route"], 16)

            a.wait_ge(S["ld_c"], 32)
            a.wait_ge(S["set_cond"], 1)
            a.activation(condT[:, :, 0], crow[:, 0, :], ACT.Silu)
            a.activation(condT[:, :, 1], crow[:, 1, :], ACT.Silu).then_inc(S["cond_ready"], 1)
            for i in range(4):
                a.wait_ge(S["ld_ctx" if i < 2 else "ld_x"], 16)
                src = ctxrow[:, i, :] if i < 2 else xrow[:, i - 2, :]
                a.activation(h2row[:, 0, :], src, ACT.Square, accum_out=sumsq[:, i:i + 1]).then_inc(S["sq_done"], 1)
                a.drain()
            a.dma_start(h2row[:, 1, :], A["norm2_g"].to_broadcast([P, D])).then_inc(S["ld_norm2"], 16)
            for n in range(8):
                i, h = n // 2, n % 2
                a.wait_ge(S["xnT_psum"], n + 1)
                a.activation(hT[:, 4 * h:4 * h + 4, P * i:P * i + P], shaped(PS[:, 4 + n % 4, :], 4, P),
                             ACT.Copy).then_inc(S["xnT_evac"], 1)
            for n, (t, is_q) in enumerate(QKV_JOBS):
                a.wait_ge(S["qkv_psum"], n + 1)
                if is_q:
                    a.activation(qk[:, t, 0:512].rearrange("p (j g d) -> p g j d", g=2, j=4),
                                 PS[:, n, :].rearrange("p (g j d) -> p g j d", g=2, j=4), ACT.Copy).then_inc(S["qkv_evac"], 1)
                else:
                    a.activation(qk[:, t, 512:640], PS[:, n, 0:128], ACT.Copy)
                    a.activation(vrow[:, t, :], PS[:, n, 128:256], ACT.Copy).then_inc(S["qkv_evac"], 1)
                    a.drain()
                    if t >= 1:
                        a.wait_ge(S["qksq_sum"], t)
                    o = 512 if t < 2 else 0
                    a.activation(qk_sq[:, o:640], qk[:, t, o:640], ACT.Square).then_inc(S["qksq_done"], 1)
            for m in range(8):
                a.wait_ge(S["gbgc_psum"], m + 1)
                dst = gbT[:, m, :] if m < 4 else gcT[:, m - 4, :]
                a.activation(dst, PS[:, 6 + m % 2, 0:TOK], ACT.Copy).then_inc(S["gbgc_evac"], 1)
            a.wait_ge(S["conv_ready"], 1)
            a.activation(sqT, yT, ACT.Square).then_inc(S["convsq_done"], 1)
            a.wait_ge(S["convms_psum"], 1)
            a.activation(flat(sqT), flat(PS[:, 6:8, :]), ACT.Sqrt, bias=eps_col).then_inc(S["convsd_done"], 1)
            for j in range(16):
                a.wait_ge(S["negmax_ready"], j + 1)
                if j >= 2:
                    a.wait_ge(S["pT_psum"], j - 1)
                a.activation(probs[:, j % 2, :], PS[:, j % 2, :], ACT.Exp, bias=negmax[:, j:j + 1], scale=HD ** -0.5,
                             accum_out=psums[:, j:j + 1]).then_inc(S["p_ready"], 1)
            for t in range(TT):
                a.wait_ge(S["x_new"], t + 1)
                a.activation(flat(probs), xrow[:, t, :], ACT.Square,
                             accum_out=sumsq[:, 4 + t:5 + t]).then_inc(S["xsq_done"], 1)
                a.drain()
            for n in range(4):
                t, h = n // 2, n % 2
                a.wait_ge(S["h2T_psum"], n + 1)
                a.activation(h2T[:, 4 * h:4 * h + 4, P * t:P * t + P], shaped(PS[:, 4 + n, :], 4, P),
                             ACT.Copy).then_inc(S["h2T_ready"], 1)
            a.wait_ge(S["gexp_in"], 1)
            a.activation(gexp, gexp, ACT.Exp).then_inc(S["gexp_out"], 1)
            a.wait_ge(S["eexp_in"], 1)
            a.activation(ed, ed, ACT.Exp).then_inc(S["eexp_out"], 1)

            def expert(it, n, h, extra_sweep=None):
                a.wait_ge(S["gu_psum"], n * 2 + (h + 1))
                a.activation(silu_g, PS[:, 2 + h, 0:192], ACT.Silu).then_inc(S["silu_ready"], 1)
                a.wait_ge(S["ye_psum"], n * 2 + (h + 1))
                a.wait_ge(y_out[h], n * 16 + 16)
                if extra_sweep is not None and h == 0:
                    a.wait_ge(S["yg_loaded"], extra_sweep * 64 + 64)
                a.activation(yexp[:, h, :], PS[:, 4 + h, 0:256], ACT.Copy)
                a.drain()
                rows = ybuf[bass.ds(it * (2 * CAP) + h * CAP, CAP)].rearrange("s (g c) -> g s c", g=4)
                a.dma_start(rows, yexp[:, h, :]).then_inc(y_out[h], 16)

            for h in range(2):
                a.sem_inc(y_out[h], 16)
            with a.Fori(0, PAIRS) as it:
                for h in range(2):
                    expert(it, it, h)
            def sweep_out(done):
                for h in range(2):
                    a.wait_ge(y_out[h], done * 16 + 16)
                a.sem_inc(S["moe_out"], 1)

            sweep_out(PAIRS)
            extra = a.value_load(extra_i[0:1, 0:1], min_val=0, max_val=SWEEPS - 1)
            with a.If(extra > 0):
                with a.Fori(0, extra) as r:
                    with a.Fori(0, PAIRS) as it:
                        for h in range(2):
                            expert(it, r * PAIRS + it + PAIRS, h, r)
                    sweep_out(r * PAIRS + 2 * PAIRS)
            a.dma_start(final_g, A["final_g"].to_broadcast([P, D])).then_inc(S["ld_final"], 16)
            a.dma_start(metarow, A["meta_tokens_2"]).then_inc(S["ld_meta"], 16)
            for t in range(TT):
                a.wait_ge(S["x1_pre"], t + 1)
                a.activation(hnrow[:, 0, :], xrow[:, t, :], ACT.Square,
                             accum_out=sumsq[:, 6 + t:7 + t]).then_inc(S["fsq_done"], 1)
                a.drain()
            a.dma_start(consts2, A["consts_c"]).then_inc(S["ld_consts2"], 16)
            a.dma_start(mixpost, A["norm_mix_post_2"].to_broadcast([P, D])).then_inc(S["ld_posts"], 16)
            a.dma_start(ffnpost, A["norm_ffn_post_2"].to_broadcast([P, D])).then_inc(S["ld_posts"], 16)

            a.wait_ge(S["ld_meta"], 16)
            a.activation(hnrow[0:META, 1, :], metarow, ACT.Square, accum_out=sumsq[0:META, 8:9]).then_inc(S["nsq_done"], 1)
            for t in range(TT):
                a.wait_ge(S["x1_ready"], t + 1)
                a.drain()
                a.activation(flat(sT)[:, 0:D], xrow[:, t, :], ACT.Square,
                             accum_out=sumsq[:, 9 + t:10 + t]).then_inc(S["nsq_done"], 1)
            for n in range(2 * RH + 1):
                h = n
                if n < RH:
                    a.wait_ge(S["v_psum"], n + 1)
                    for t in range(TT):
                        a.activation(vbuf[:, n % 2, t, :], PS[:, t, :], ACT.Copy)
                    a.activation(vmbuf[0:META, n % 2, :], PS[0:META, 2, :], ACT.Copy).then_inc(S["v_evac"], 1)
                    a.wait_ge(S["rg_psum"], n + 1)
                    if n == 0:
                        a.wait_ge(S["hn_ready"], 1)
                    a.activation(yr[:, n % 2].rearrange("p t n -> p (t n)"), flat(PS[:, 3:5, :]), ACT.Silu)\
                        .then_inc(S["rg_silu"], 1)
                if 1 <= n <= RH:
                    for t in range(TT):
                        k = TT * (n - 1) + t
                        a.wait_ge(S["yrT_psum"], k + 1)
                        a.activation(yrT[:, 4 * (n - 1):4 * n, P * t:P * t + P], shaped(PS[:, 7, :], 4, P),
                                     ACT.Copy).then_inc(S["yrT_evac"], 1)
            for m in range(2 * KD):
                a.wait_ge(S["sqk_psum"], m + 1)
                if m < KD:
                    a.activation(qR[:, m, :], PS[:, m % 4, 0:TOK], ACT.Copy, scale=HD ** -0.5).then_inc(S["sqk_evac"], 1)
                else:
                    a.activation(kR[:, m - KD, :], PS[:, m % 4, 0:LK], ACT.Copy).then_inc(S["sqk_evac"], 1)
            for i in range(2):
                a.wait_ge(S["sv_psum"], i + 1)
                for t in range(TT):
                    a.activation(vS[:, t, CW * i:CW * i + CW], PS[:, 4 + t, :], ACT.Copy)
                a.activation(vmS[0:META, CW * i:CW * i + CW], PS[0:META, 6, :], ACT.Copy).then_inc(S["sv_evac"], 1)
            a.drain()
            for gg in range(1, 4):
                a.dma_start(vmS[32 * gg:32 * gg + META, :], vmS[0:META, :]).then_inc(S["vm_copied"], 16)

            def softplus_tail(dst, src):
                a.activation(dst, src, ACT.Abs)
                a.drain()
                a.activation(dst, dst, ACT.Exp, scale=-1.0)
                a.drain()
                return a.activation(dst, dst, ACT.Ln, bias=1.0)

            for n in range(SH + 1):
                if n < SH:
                    if n % 4 == 0:
                        a.wait_ge(S["mz_psum"], n // 4 + 1)
                        if n:
                            a.wait_ge(S["cum_psum"], n)
                        softplus_tail(Lm, PS[:, 3 + n // 4 % 2, 0:TOK]).then_inc(S["splm_done"], 1)
                    a.wait_ge(S["z_psum"], n + 1)
                    if n >= 3:
                        a.wait_ge(S["cum_psum"], n - 2)
                    softplus_tail(EL[:, n % 3, :], PS[:, SB_BANKS[n % 4], 0:DIAG]).then_inc(S["spl_done"], 1)
                if n >= 1:
                    j = n - 1
                    a.wait_ge(S["arg_done"], j + 1)
                    a.activation(aT[:, j % 6, :], aT[:, j % 6, :], ACT.Exp).then_inc(S["aT_ready"], 1)
                    if j % 4 == 3:
                        G = j // 4
                        a.wait_ge(S["cum_psum"], j + 1)
                        a.activation(aTm[:, G % 2, :], PS[:, 3 + G % 2, 0:TOK], ACT.Exp).then_inc(S["aTm_ready"], 1)
                    if j % 4 == 1 and j > 4:
                        evac_sb(a, j // 4 - 1)
            evac_sb(a, 3)
            for q in range(4):
                a.wait_ge(S["quad_psum"], q + 1)
                if q >= 1:
                    a.wait_ge(S["merge_done"], q)
                b = 4 * (q % 2) + 2
                a.activation(gsig[:, 0:D], flat(PS[:, b:b + 2, :]), ACT.Sigmoid).then_inc(S["quad_sig"], 1)
            a.wait_ge(S["mix_psum"], 2)
            a.drain()
            for t in range(TT):
                a.activation(gsig[:, 0:D], flat(PS[:, 2 * t:2 * t + 2, :]), ACT.Square,
                             accum_out=sumsq[:, 11 + t:12 + t]).then_inc(S["mixsq_done"], 1)
                a.drain()
            for t in range(TT):
                a.wait_ge(S["h_ready"], t + 1)
                a.activation(flat(sT)[:, 0:D], xrow[:, t, :], ACT.Square,
                             accum_out=sumsq[:, 8 + t:9 + t]).then_inc(S["nsq_done"], 1)
                a.drain()
            for j in range(FB // 2):
                a.wait_ge(S["ff_psum"], j + 1)
                if j >= 2:
                    a.wait_ge(S["ff_ready"], j - 1)
                a.activation(ff_tmp[:, j % 2, :], PS[:, 2 * (j % 2), :], ACT.Silu).then_inc(S["ff_silu"], 1)
            a.wait_ge(S["fo_psum"], -(-FB // 4))
            a.drain()
            for t in range(TT):
                a.activation(gsig[:, 0:D], flat(PS[:, 4 + 2 * t:6 + 2 * t, :]), ACT.Square,
                             accum_out=sumsq[:, 13 + t:14 + t]).then_inc(S["fosq_done"], 1)
                a.drain()
            for t in range(TT):
                a.wait_ge(S["out_ready"], t + 1)
                a.dma_start(out[P * t:P * t + P, :], xrow[:, t, :]).then_inc(S["out_done"], 16)
            a.wait_ge(S["out_done"], 32)

        @block.vector
        def _(v):
            def wide(ap, *shape):
                return ap.unsqueeze(len(ap.shape)).to_broadcast([P, *shape])

            for i in range(4):
                src = ctxrow[:, i, :] if i < 2 else xrow[:, i - 2, :]
                v.wait_ge(S["rstd_done"], i + 1)
                if i >= 2:
                    v.wait_ge(S["xnT_psum"], 2 * (i - 1))
                v.tensor_scalar(xn[:, i % 2, :], src, rstd[:, i:i + 1], None, ALU.mult).then_inc(S["xn_ready"], 1)
            v.wait_ge(S["vec_psum"], 1)
            v.tensor_copy(vecT, PS[:, 0, 0:VEC_N]).then_inc(S["vec_ready"], 1)

            def mod_rows(n0, n1, bank0):
                for n in range(n0, n1, 2):
                    k = min(2, n1 - n)
                    last = v.tensor_tensor(modrow[:, n - n0:n - n0 + k, :],
                                           shaped(PS[:, bank0 + (n - n0) // 2, 0:192 * k], k, 192),
                                           bias[:, n:n + k, :], ALU.add)
                return last

            v.wait_ge(S["ld_bias"], 128)
            v.wait_ge(S["mod_psum"], 3)
            mod_rows(0, 3, 1).then_inc(S["modA_rows"], 1)
            v.wait_ge(S["vec2_psum"], 1)
            for r in range(2):
                v.scalar_tensor_tensor(mods[:, r, 0:8], PS[:, 3, 16 * r + 8:16 * r + 16], 1.0, V["norm1_g"],
                                       ALU.add, ALU.mult)
                v.tensor_copy(mods[:, r, 8:16], PS[:, 3, 16 * r:16 * r + 8])
            v.wait_ge(S["xnT_evac"], 8)
            v.drain()
            for c in range(KD):
                for r, cols_ in ((1, slice(0, TOK)), (0, slice(TOK, 2 * TOK))):
                    last = v.tensor_scalar(hT[:, c, cols_], hT[:, c, cols_], mods[:, r, c:c + 1], mods[:, r, 8 + c:9 + c],
                                           ALU.mult, ALU.add)
            last.then_inc(S["hT_ready"], 1)

            v.wait_ge(S["ld_headg"], 32)
            for t in range(4):
                lo, n = (8, 2) if t < 2 else (0, 10)
                rows = shaped(qk[:, t, 64 * lo:640], n, HD)
                v.wait_ge(S["qksq_done"], t + 1)
                v.reduce_sum(hss[:, 0:n], shaped(qk_sq[:, 64 * lo:640], n, HD), AX).then_inc(S["qksq_sum"], 1)
                if lo == 0:
                    v.tensor_tensor(rows[:, 0:8, :], rows[:, 0:8, :], headg[:, 0:64].unsqueeze(1).to_broadcast([P, 8, HD]), ALU.mult)
                kk = rows[:, n - 2:n, :]
                v.tensor_tensor(kk, kk, headg[:, 64:128].unsqueeze(1).to_broadcast([P, 2, HD]), ALU.mult)
                v.wait_ge(S["qk_rstd"], t + 1)
                v.drain()
                last = v.tensor_tensor(rows, rows, wide(hrs[:, 0:n], n, HD), ALU.mult)
                if lo == 0:
                    v.drain()
                    parts = qk[:, t, :].rearrange("p (n a u f) -> p n a u f", n=10, a=2, u=2)
                    for ax in range(2):
                        x1, x2 = parts[:, :, ax, 0, :], parts[:, :, ax, 1, :]
                        o = 32 * (t - 2) + 16 * ax
                        cos = K["rope_cos"][:, o:o + 16].unsqueeze(1).to_broadcast([P, 10, 16])
                        sin = K["rope_sin"][:, o:o + 16].unsqueeze(1).to_broadcast([P, 10, 16])
                        tmp = [shaped(rope_tmp[:, 160 * i:160 * i + 160], 10, 16) for i in range(4)]
                        v.tensor_tensor(tmp[0], x1, cos, ALU.mult)
                        v.tensor_tensor(tmp[1], x2, sin, ALU.mult)
                        v.tensor_tensor(tmp[2], x1, sin, ALU.mult)
                        v.tensor_tensor(tmp[3], x2, cos, ALU.mult)
                        v.drain()
                        v.tensor_tensor(x1, tmp[0], tmp[1], ALU.subtract)
                        last = v.tensor_tensor(x2, tmp[2], tmp[3], ALU.add)
                        v.drain()
                last.then_inc(S["qk_ready"], 1)

            v.memset(vTc[:, :, 0:1], 0.0)
            v.memset(vTc[:, :, TOK + 1:TOK + 2], 0.0)
            for m in range(CV):
                v.wait_ge(S["gbgc_evac"], CV + m + 1)
                v.wait_ge(S["u_psum"], m + 1)
                v.tensor_tensor(vTc[:, m, 1:TOK + 1], gcT[:, m, :], PS[:, 6 + m % 2, 0:TOK], ALU.mult).then_inc(S["u_evac"], 1)
                v.drain()
                v.tensor_scalar(yT[:, m, :], vTc[:, m, 0:TOK], V["conv_w"][:, m:m + 1], None, ALU.mult)
                for k in (1, 2):
                    v.drain()
                    v.scalar_tensor_tensor(yT[:, m, :], vTc[:, m, k:k + TOK], V["conv_w"][:, 4 * k + m:4 * k + m + 1],
                                           yT[:, m, :], ALU.mult, ALU.add)
                v.drain()
                last = v.tensor_tensor(yT[:, m, :], yT[:, m, :], gbT[:, m, :], ALU.mult)
            last.then_inc(S["conv_ready"], 1)

            v.wait_ge(S["mod_psum"], 8)
            mod_rows(3, 8, 0).then_inc(S["modB_rows"], 1)

            v.wait_ge(S["qkT_psum"], 3)
            for t in range(TT):
                v.tensor_copy(qT[:, :, P * t:P * t + P], shaped(PS[:, 3 + t, :], 4, P))
            v.tensor_copy(kT, PS[:, 5, :]).then_inc(S["qkT_ready"], 1)

            v.wait_ge(S["convsd_done"], 1)
            v.reciprocal(flat(sqT), flat(sqT))
            v.drain()
            for m in range(CV):
                last = v.scalar_tensor_tensor(mixT[:, CV + m, :], yT[:, m, :], V["conv_out_g"][:, m:m + 1], sqT[:, m, :],
                                              ALU.mult, ALU.mult)
            last.then_inc(S["conv_done"], 1)

            def row_max(j):
                v.wait_ge(S["s_psum"], j + 1)
                v.reduce_max(mx[:, j:j + 1], PS[:, j % 2, :], AX)
                v.drain()
                v.tensor_scalar(negmax[:, j:j + 1], mx[:, j:j + 1], -HD ** -0.5, None, ALU.mult).then_inc(S["negmax_ready"], 1)

            row_max(0)
            for j in range(16):
                if j < 15:
                    row_max(j + 1)
                v.wait_ge(S["pT_psum"], j + 1)
                if j >= 2:
                    v.wait_ge(S["pv_psum"], j - 1)
                v.tensor_copy(pT[:, j % 2], shaped(PS[:, 2 + j % 2, :], 4, P)).then_inc(S["pT_ready"], 1)
                if j % 8 == 7:
                    t = j // 8
                    rows = shaped(arow[:, t, :], 8, HD)
                    v.reciprocal(precip[:, 8 * t:8 * t + 8], psums[:, 8 * t:8 * t + 8])
                    v.wait_ge(S["pv_psum"], j + 1)
                    v.drain()
                    v.tensor_tensor(rows, shaped(PS[:, 4 + t, :], 8, HD), wide(precip[:, 8 * t:8 * t + 8], 8, HD), ALU.mult)
                    v.drain()
                    v.wait_ge(S["modB_out"], 64)
                    v.tensor_tensor(qk_sq[:, 0:512], arow[:, t, :], arow[:, t, :], ALU.mult)
                    v.drain()
                    v.reduce_sum(hss[:, 0:8], shaped(qk_sq[:, 0:512], 8, HD), AX).then_inc(S["a_sum"], 1)
                    v.wait_ge(S["a_rstd"], t + 1)
                    v.tensor_tensor(rows, rows, wide(hrs[:, 0:8], 8, HD), ALU.mult).then_inc(S["a_ready"], 1)
            for t in range(TT):
                v.wait_ge(S["aT_psum"], t + 1)
                for m in range(4):
                    last = v.tensor_scalar(mixT[:, m, P * t:P * t + P], PS[:, 6 + t, P * m:P * m + P],
                                           V["attn_out_g"][:, m:m + 1], None, ALU.mult)
                last.then_inc(S["mixT_ready"], 1)

            v.wait_ge(S["ld_rowmods"], 64)
            v.wait_ge(S["ld_norm2"], 16)
            v.scalar_tensor_tensor(scale2, scale2, 1.0, h2row[:, 1, :], ALU.add, ALU.mult)
            for o in range(2):
                for t in range(TT):
                    n = 2 * o + t
                    part = slice(CW * o, CW * o + CW)
                    v.wait_ge(S["xo_psum"], n + 1)
                    v.tensor_tensor(arow[:, t, :], PS[:, n, :], gate1[:, part], ALU.mult)
                    v.drain()
                    last = v.tensor_tensor(xrow[:, t, part], xrow[:, t, part], arow[:, t, :], ALU.add)
                    if o == 1:
                        last.then_inc(S["x_new"], 1)
            for t in range(TT):
                v.wait_ge(S["x_rstd"], t + 1)
                v.drain()
                v.scalar_tensor_tensor(h2row[:, t, :], xrow[:, t, :], rstd[:, 4 + t:5 + t], scale2, ALU.mult, ALU.mult)
                v.drain()
                v.tensor_tensor(h2row[:, t, :], h2row[:, t, :], shift2, ALU.add).then_inc(S["h2_ready"], 1)

            v.wait_ge(S["logit_psum"], 1)
            v.tensor_copy(logits, shaped(PS[:, 0, 0:TT * (EG + E)], TT, EG + E))
            v.drain()
            lg, le = logits[:, :, 0:EG], logits[:, :, EG:EG + E].rearrange("p t (g e) -> p t g e", g=EG)
            v.reduce_max(gmax, lg, AX)
            v.drain()
            v.tensor_tensor(gexp, lg, wide(gmax, TT, EG), ALU.subtract).then_inc(S["gexp_in"], 1)
            v.tensor_tensor(goh, lg, wide(gmax, TT, EG), ALU.is_equal)
            v.drain()
            v.scalar_tensor_tensor(gcand, goh, -8.0, K["iota4p8"].unsqueeze(1).to_broadcast([P, TT, EG]), ALU.mult, ALU.add)
            v.drain()
            v.tensor_reduce(gsel, gcand, AX, ALU.min)
            v.drain()
            v.tensor_tensor(goh, K["iota4"].unsqueeze(1).to_broadcast([P, TT, EG]), wide(gsel, TT, EG), ALU.is_equal)
            v.drain()
            v.tensor_scalar(gcand, goh, BIG, -BIG, ALU.mult, ALU.add)
            em = emask.rearrange("p t (g e) -> p t g e", g=EG)
            for t in range(TT):
                v.tensor_tensor(em[:, t], le[:, t], wide(goh[:, t], EG, E // EG), ALU.mult)
            v.drain()
            for t in range(TT):
                v.tensor_tensor(em[:, t], em[:, t], wide(gcand[:, t], EG, E // EG), ALU.add)
            v.drain()
            for t in range(TT):
                v.max(top8[:, t, :], emask[:, t, :])
            v.drain()
            v.tensor_tensor(ed, top8[:, :, 1], top8[:, :, 0], ALU.subtract).then_inc(S["eexp_in"], 1)
            for t in range(TT):
                v.max_index(top_idx[:, t, :], top8[:, t, :], emask[:, t, :])
            v.drain()
            v.tensor_copy(top_e, top_idx[:, :, 0:2])
            v.drain()
            for t in range(TT):
                v.tensor_tensor(onehot[:, t], K["iota"].unsqueeze(1).to_broadcast([P, 2, E]), wide(top_e[:, t], 2, E), ALU.is_equal)
            v.drain()
            v.tensor_tensor(chosen, onehot[:, :, 0, :], onehot[:, :, 1, :], ALU.add).then_inc(S["onehot_ready"], 1)
            v.wait_ge(S["gexp_out"], 1)
            v.reduce_sum(gsum, gexp, AX)
            v.wait_ge(S["eexp_out"], 1)
            v.drain()
            v.scalar_tensor_tensor(den, ed, 1.0, gsum, ALU.add, ALU.mult)
            v.drain()
            v.reciprocal(wts[:, :, 0], den)
            v.drain()
            v.tensor_tensor(wts[:, :, 1], wts[:, :, 0], ed, ALU.mult)
            v.wait_ge(S["rank_psum"], 1)
            v.tensor_copy(rank, shaped(PS[:, 2, 0:TT * E], TT, E))
            v.tensor_copy(counts, PS[:, 3, 0:E])
            v.drain()
            v.scalar_tensor_tensor(posadj, rank, 1.0, chosen, ALU.add, ALU.mult)
            for t in range(TT):
                v.tensor_tensor(oh_rank[:, t], onehot[:, t], rank[:, t].unsqueeze(1).to_broadcast([P, 2, E]), ALU.mult)
            v.reduce_max(maxc, counts, AX)
            v.drain()
            v.tensor_scalar(posadj, posadj, -1.0, None, ALU.add)
            v.tensor_copy(iota_r, K["iota"])
            v.reduce_sum(rank_e, oh_rank, AX)
            v.tensor_tensor(hit7, maxc.to_broadcast([P, 7]), K["steps7"], ALU.is_gt)
            v.drain()
            v.reduce_sum(extra_f, hit7, AX)
            for t in range(TT):
                v.tensor_tensor(steps_hit[:, 2 * t:2 * t + 2, :], wide(rank_e[:, t], 2, 7),
                                K["steps7"].unsqueeze(1).to_broadcast([P, 2, 7]), ALU.is_ge)
            v.drain()
            v.tensor_copy(extra_i[:, :], extra_f)
            v.reduce_sum(flat(sweep_e), steps_hit, AX)
            v.memset(sweep_now, 0.0)
            v.memset(flat(mixT), 0.0)
            v.drain()
            v.scalar_tensor_tensor(ids_f, sweep_e, -float(CAP), rank_e, ALU.mult, ALU.add)
            v.drain()
            v.scalar_tensor_tensor(ids_f, top_e, float(CAP), ids_f, ALU.mult, ALU.add)
            v.drain()
            v.tensor_copy(row_ids[:, :, :], ids_f)
            v.drain().then_inc(S["route_ready"], 1)

            def expert(it, n, h):
                for t in range(TT):
                    last = v.tensor_scalar(pick[:, h, t, :], iota_r, posadj[:, t, bass.ds(it * 2 + h, 1)], None,
                                           ALU.is_equal)
                last.then_inc(S["pick_ready"], 1)
                v.wait_ge(S["xe_psum"], n * 2 + (h + 1))
                v.transpose(xTe[:, h], PS[:, h, 0:256].rearrange("p (q j) -> p j q", j=KD)).then_inc(S["xe_ready"], 1)
                v.wait_ge(S["silu_ready"], n * 2 + (h + 1))
                v.tensor_tensor(hmid, silu_g, PS[:, 2 + h, 192:384], ALU.mult)
                v.drain()
                v.transpose(hTe[:, h], hmid.rearrange("p (q j) -> p j q", j=JE)).then_inc(S["he_ready"], 1)

            with v.Fori(0, PAIRS) as it:
                for h in range(2):
                    expert(it, it, h)
            def accumulate(loads):
                v.scalar_tensor_tensor(wts_now, sweep_e, sweep_now, wts, ALU.is_equal, ALU.mult)
                v.drain()
                v.wait_ge(S["yg_loaded"], loads)
                for k in range(2):
                    for t in range(TT):
                        v.scalar_tensor_tensor(moe[:, t, :], ygat[t][k], wts_now[:, t, k:k + 1], moe[:, t, :],
                                               ALU.mult, ALU.add)
                    v.drain()

            accumulate(64)
            extra = v.value_load(extra_i[0:1, 0:1], min_val=0, max_val=SWEEPS - 1)
            with v.If(extra > 0):
                with v.Fori(0, extra) as r:
                    v.tensor_scalar(iota_r, iota_r, float(CAP), None, ALU.add)
                    v.tensor_scalar(sweep_now, sweep_now, 1.0, None, ALU.add)
                    v.drain()
                    with v.Fori(0, PAIRS) as it:
                        for h in range(2):
                            expert(it, r * PAIRS + it + PAIRS, h)
                    accumulate(r * 64 + 128)

            for t in range(TT):
                v.tensor_tensor(moe[:, t, :], moe[:, t, :], gate2, ALU.mult)
                v.drain()
                v.tensor_tensor(xrow[:, t, :], xrow[:, t, :], moe[:, t, :], ALU.add).then_inc(S["x1_pre"], 1)
            v.wait_ge(S["ld_final"], 16)
            for t in range(TT):
                v.wait_ge(S["f_rstd"], t + 1)
                v.drain()
                v.scalar_tensor_tensor(xrow[:, t, :], xrow[:, t, :], rstd[:, 6 + t:7 + t], final_g, ALU.mult, ALU.mult)\
                    .then_inc(S["x1_ready"], 1)

            def normed_T(n_psum, rows, gain, dst, bank, blocks, width):
                v.wait_ge(S["hnT_psum"], n_psum)
                return v.tensor_tensor(dst, shaped(PS[:, bank, 0:blocks * width], blocks, width),
                                       wide(gain, blocks, width), ALU.mult)

            v.wait_ge(S["n_rstd"], 1)
            v.tensor_scalar(hnrow[0:META, 0, :], metarow, rstd[0:META, 8:9], None, ALU.mult).then_inc(S["hn_ready"], 1)
            for t in range(TT):
                v.wait_ge(S["n_rstd"], 2 + t)
                if t == 1:
                    v.wait_ge(S["hnT_psum"], 1)
                v.tensor_scalar(hnrow[:, 1 - t, :], xrow[:, t, :], rstd[:, 9 + t:10 + t], None, ALU.mult)\
                    .then_inc(S["hn_ready"], 1)
            gain = V["norm_mix_pre_2"]
            normed_T(1, META, gain, hnT[:, :, 0:META], 0, KD, META)
            for n in range(4):
                t, h = n // 2, n % 2
                last = normed_T(2 + n, P, gain[:, 4 * h:4 * h + 4],
                                hnT[:, 4 * h:4 * h + 4, META + P * t:META + P * t + P], 1 + n, 4, P)
            last.then_inc(S["hnT_ready"], 1)

            v.wait_ge(S["ld_consts2"], 16)
            for n in range(2 * RH):
                h, w = n % RH, TOK if n < RH else LK
                dst = qR if n < RH else kR
                b = 2 * (n % 2)
                cos, sin = K2["cos"][:, LK - w:LK], K2["sin"][:, LK - w:LK]
                x1, x2 = PS[:, b, 0:w], PS[:, b + 1, 0:w]
                tmp = [rot_tmp[:, LK * i:LK * i + w] for i in range(4)]
                v.wait_ge(S["rqk_psum"], n + 1)
                v.tensor_tensor(tmp[0], x1, cos, ALU.mult)
                v.tensor_tensor(tmp[1], x2, sin, ALU.mult)
                v.tensor_tensor(tmp[2], x1, sin, ALU.mult)
                v.tensor_tensor(tmp[3], x2, cos, ALU.mult)
                v.drain()
                v.tensor_tensor(dst[:, 2 * h, 0:w], tmp[0], tmp[1], ALU.subtract)
                v.tensor_tensor(dst[:, 2 * h + 1, 0:w], tmp[2], tmp[3], ALU.add).then_inc(S["rot_done"], 1)
                v.drain()
            for h in range(RH):
                v.wait_ge(S["rs_psum"], h + 1)
                v.tensor_tensor(sT[:, h, :], PS[:, 4 + h % 2, 0:DIAG], K2["decay"][:, DIAG * h:DIAG * h + DIAG], ALU.mult)
                v.tensor_tensor(sTm[0:META, h, :], PS[0:META, 6 + h % 2, 0:TOK],
                                K2["decay_meta"][0:META, TOK * h:TOK * h + TOK], ALU.mult).then_inc(S["rs_ready"], 1)
            for h in range(RH):
                v.wait_ge(S["y_psum"], h + 1)
                for t in range(TT):
                    v.bn_stats(bn[:, t, :], PS[:, 5 + t, :])
                v.drain()
                for t in range(TT):
                    v.bn_aggr(mv[:, t, :], bn[:, t, :])
                v.drain().then_inc(S["y_var"], 1)
                v.wait_ge(S["y_rstd"], h + 1)
                for t in range(TT):
                    v.tensor_scalar(gn_tmp[:, RDV * t:RDV * t + RDV], PS[:, 5 + t, :], mv[:, t, 0:1], mv[:, t, 1:2],
                                    ALU.subtract, ALU.mult)
                v.wait_ge(S["rg_silu"], h + 1)
                v.drain()
                yh = yr[:, h % 2].rearrange("p t n -> p (t n)")
                v.tensor_tensor(yh, yh, gn_tmp, ALU.mult).then_inc(S["yr_ready"], 1)

            for n in range(SH + 1):
                if n < SH:
                    if n % 4 == 0:
                        v.wait_ge(S["splm_done"], n // 4 + 1)
                        v.scalar_tensor_tensor(Lm, PS[:, 3 + n // 4 % 2, 0:TOK], 0.0, Lm, ALU.max, ALU.add).then_inc(S["Lm_ready"], 1)
                    v.wait_ge(S["spl_done"], n + 1)
                    L = EL[:, n % 3, :]
                    v.scalar_tensor_tensor(L, PS[:, SB_BANKS[n % 4], 0:DIAG], 0.0, L, ALU.max, ALU.add)
                    v.drain()
                    for o in (0, TOK):
                        last = v.tensor_tensor(L[:, o:o + P], L[:, o:o + P], K2["valid"], ALU.mult)
                    last.then_inc(S["L_ready"], 1)
                if n >= 1:
                    j = n - 1
                    v.wait_ge(S["cum_psum"], j + 1)
                    v.scalar_tensor_tensor(aT[:, j % 6, :], PS[:, SB_BANKS[j % 4], 0:DIAG], 0.0, K2["invalid"],
                                           ALU.min, ALU.add).then_inc(S["arg_done"], 1)

            for q in range(4):
                half = q % 2
                dst = flat(merged[:, 4 * half:4 * half + 4, :])
                b = 4 * (q % 2)
                src = flat(PS[:, b:b + 2, :])
                v.wait_ge(S["quad_sig"], q + 1)
                if q < 2:
                    v.tensor_tensor(dst, gsig[:, 0:D], src, ALU.mult).then_inc(S["merge_done"], 1)
                else:
                    v.tensor_tensor(gsig[:, D:2 * D], gsig[:, 0:D], src, ALU.mult)
                    v.drain()
                    v.tensor_tensor(dst, dst, gsig[:, D:2 * D], ALU.add).then_inc(S["merge_done"], 1)

            def post_norm(rstd_sem, col, bank, gain, done):
                for t in range(TT):
                    v.wait_ge(S[rstd_sem], t + 1)
                    v.scalar_tensor_tensor(gsig[:, D:2 * D], flat(PS[:, bank + 2 * t:bank + 2 * t + 2, :]),
                                           rstd[:, col + t:col + t + 1], gain, ALU.mult, ALU.mult)
                    v.drain()
                    v.tensor_tensor(xrow[:, t, :], xrow[:, t, :], gsig[:, D:2 * D], ALU.add).then_inc(S[done], 1)
                    v.drain()

            v.wait_ge(S["ld_posts"], 32)
            post_norm("mix_rstd", 11, 0, mixpost, "h_ready")
            for t in range(TT):
                v.wait_ge(S["n_rstd"], 4 + t)
                v.tensor_scalar(hnrow[:, t, :], xrow[:, t, :], rstd[:, 8 + t:9 + t], None, ALU.mult).then_inc(S["hn_ready"], 1)
            gain = V["norm_ffn_pre_2"]
            for n in range(4):
                t, h = n // 2, n % 2
                last = normed_T(6 + n, P, gain[:, 4 * h:4 * h + 4], hnT[:, 4 * h:4 * h + 4, P * t:P * t + P], 4 + n, 4, P)
            last.then_inc(S["hnT_ready"], 1)
            for j in range(FB // 2):
                v.wait_ge(S["ff_silu"], j + 1)
                v.tensor_tensor(flat(gT[:, 2 * j:2 * j + 2, :]), ff_tmp[:, j % 2, :], PS[:, 2 * (j % 2) + 1, :], ALU.mult)\
                    .then_inc(S["ff_ready"], 1)
            post_norm("fo_rstd", 13, 4, ffnpost, "out_ready")

        @block.tensor
        def _(pe):
            mm = pe.matmul

            def rows_of(bank, w, lhs, n, col0=0, m=P):
                for c in range(KD):
                    last = mm(PS[0:m, bank, 0:n], lhs(c), w[:, c, col0:col0 + n], start=c == 0, stop=c == KD - 1)
                return last

            def transposes(bank, srcs, rows=P):
                for i, s in enumerate(srcs):
                    last = pe.transpose(PS[:, bank, rows * i:rows * i + rows], s, ident[0:rows, 0:rows])
                return last

            pe.wait_ge(S["ld_consts"], 16)
            pe.wait_ge(S["ld_vec"], 16 * len(VEC))
            pe.transpose(PS[:, 0, 0:VEC_N], vec, ident[0:VEC_N, 0:VEC_N]).then_inc(S["vec_psum"], 1)
            for n in range(8):
                i, h = n // 2, n % 2
                pe.wait_ge(S["xn_ready"], i + 1)
                if n >= 4:
                    pe.wait_ge(S["xnT_evac"], n - 3)
                transposes(4 + n % 4, [xn[:, i % 2, P * c:P * c + P] for c in range(4 * h, 4 * h + 4)])\
                    .then_inc(S["xnT_psum"], 1)

            def modulate(n, bank, col):
                chunk_landed(pe, CHUNK_OF_MOD[n])
                w = chunk(CHUNK_OF_MOD[n])
                for c in range(KD):
                    for gg in range(4):
                        last = mm(PS[32 * gg:32 * gg + 32, bank, col:col + 192], condT[:, c, :],
                                  w[:, c, 192 * gg:192 * gg + 192], start=c == 0, stop=c == KD - 1, skip_group_check=True)
                last.then_inc(S["mod_psum"], 1)

            CHUNK_OF_MOD = [0, 1, 2] + list(range(MODB, MODB + 5))
            pe.wait_ge(S["cond_ready"], 1)
            for n in range(3):
                modulate(n, 1 + n // 2, 192 * (n % 2))
            pe.wait_ge(S["ld_vec2"], 32)
            pe.transpose(PS[:, 3, 0:32], vec2, ident[0:32, 0:32]).then_inc(S["vec2_psum"], 1)

            pe.wait_ge(S["hT_ready"], 1)
            chunk_landed(pe, WIN)
            for n, (t, is_q) in enumerate(QKV_JOBS):
                last = rows_of(n, chunk(WIN), lambda c: hT[:, c, P * t:P * t + P], 512 if is_q else 256,
                               0 if is_q else 512)
                last.then_inc(S["qkv_psum"], 1)
            for m in range(3 * CV):
                w = chunk(WIN + 1 + m // 6)
                if m % 6 == 0:
                    chunk_landed(pe, WIN + 1 + m // 6)
                if m >= 2:
                    if m - 2 < 2 * CV:
                        pe.wait_ge(S["gbgc_evac"], m - 1)
                    else:
                        pe.wait_ge(S["u_evac"], m - 2 - 2 * CV + 1)
                for c in range(KD):
                    last = mm(PS[:, 6 + m % 2, 0:TOK], w[:, c, P * (m % 6):P * (m % 6) + P], hT[:, c, TOK:2 * TOK],
                              start=c == 0, stop=c == KD - 1)
                last.then_inc(S["gbgc_psum"] if m < 2 * CV else S["u_psum"], 1)
            pe.wait_ge(S["qkv_evac"], 6)
            for n in range(3, 8):
                modulate(n, (n - 3) // 2, 192 * ((n - 3) % 2))
            for t in range(TT):
                pe.wait_ge(S["qk_ready"], 3 + t)
                transposes(3 + t, [qk[:, 2 + t, P * j:P * j + P] for j in range(4)]).then_inc(S["qkT_psum"], 1)
            transposes(5, [qk[:, i, 512:640] for i in range(4)]).then_inc(S["qkT_psum"], 1)
            pe.wait_ge(S["convsq_done"], 1)
            for b in range(2):
                last = mm(PS[:, 6 + b, :], K["headmean"], flat(sqT)[:, 512 * b:512 * b + 512], start=True, stop=True)
            last.then_inc(S["convms_psum"], 1)

            pe.wait_ge(S["qkT_ready"], 1)
            pe.wait_ge(S["modB_rows"], 1)

            def scores(j):
                t, h = j // 8, j % 8
                g0 = 64 * (h // 4)
                if j >= 2:
                    pe.wait_ge(S["p_ready"], j - 1)
                mm(PS[:, j % 2, :], qT[g0:g0 + 64, h % 4, P * t:P * t + P], kT[g0:g0 + 64, :], start=True, stop=True)\
                    .then_inc(S["s_psum"], 1)

            def weighted(j):
                t, h = j // 8, j % 8
                pe.wait_ge(S["pT_ready"], j + 1)
                for b in range(4):
                    last = mm(PS[:, 4 + t, HD * h:HD * h + HD], pT[:, j % 2, b, :], vrow[:, b, 64 * (h // 4):64 * (h // 4) + 64],
                              start=b == 0, stop=b == 3, skip_group_check=True)
                last.then_inc(S["pv_psum"], 1)

            scores(0)
            for j in range(17):
                if j < 15:
                    scores(j + 1)
                if j < 16:
                    pe.wait_ge(S["p_ready"], j + 1)
                    if j >= 2:
                        pe.wait_ge(S["pT_ready"], j - 1)
                    transposes(2 + j % 2, [probs[:, j % 2, P * b:P * b + P] for b in range(4)]).then_inc(S["pT_psum"], 1)
                if j >= 1:
                    weighted(j - 1)
            pe.wait_ge(S["convsd_done"], 1)
            for t in range(TT):
                pe.wait_ge(S["a_ready"], t + 1)
                transposes(6 + t, [arow[:, t, P * m:P * m + P] for m in range(4)]).then_inc(S["aT_psum"], 1)

            pe.wait_ge(S["mixT_ready"], TT)
            pe.wait_ge(S["conv_done"], 1)
            for o in range(2):
                chunk_landed(pe, WOUT + o)
                for t in range(TT):
                    last = rows_of(2 * o + t, chunk(WOUT + o), lambda c: mixT[:, c, P * t:P * t + P], CW)
                    last.then_inc(S["xo_psum"], 1)
            for n in range(4):
                t, h = n // 2, n % 2
                pe.wait_ge(S["h2_ready"], t + 1)
                transposes(4 + n, [h2row[:, t, P * c:P * c + P] for c in range(4 * h, 4 * h + 4)]).then_inc(S["h2T_psum"], 1)
            pe.wait_ge(S["ld_route"], 32)
            pe.wait_ge(S["h2T_ready"], 4)
            NR = EG + E
            for t in range(TT):
                for c in range(KD):
                    last = mm(PS[:, 0, NR * t:NR * t + NR], h2T[:, c, P * t:P * t + P], w_route[:, c, :],
                              start=c == 0, stop=c == KD - 1, skip_group_check=True)
            last.then_inc(S["logit_psum"], 1)
            pe.wait_ge(S["onehot_ready"], 1)
            mm(PS[:, 2, 0:E], K["before"], chosen[:, 0, :], start=True, stop=True)
            mm(PS[:, 2, E:2 * E], K["ones"], chosen[:, 0, :], start=True, stop=False)
            mm(PS[:, 2, E:2 * E], K["before"], chosen[:, 1, :], start=False, stop=True)
            mm(PS[:, 3, 0:E], K["ones"], chosen[:, 0, :], start=True, stop=False)
            mm(PS[:, 3, 0:E], K["ones"], chosen[:, 1, :], start=False, stop=True).then_inc(S["rank_psum"], 1)
            pe.wait_ge(S["route_ready"], 1)

            def expert(n, h):
                pe.wait_ge(S["pick_ready"], n * 2 + (h + 1))
                for t in range(TT):
                    for gg in range(4):
                        last = mm(PS[32 * gg:32 * gg + 32, h, 0:256], pick[:, h, t, :], h2row[:, t, 256 * gg:256 * gg + 256],
                                  start=t == 0, stop=t == TT - 1, skip_group_check=True)
                last.then_inc(S["xe_psum"], 1)
                pe.wait_ge(S["xe_ready"], n * 2 + (h + 1))
                for j in range(2):
                    pe.wait_ge(w_full[3 * h + j], n * 16 + (16 * used[3 * h + j] + 16))
                for c in range(KD):
                    for gg in range(4):
                        o = FE * c + 192 * gg
                        last = mm(PS[32 * gg:32 * gg + 32, 2 + h, 0:384], xTe[:, h, c, :],
                                  slots[:, 3 * h:3 * h + 2, o:o + 192], start=c == 0, stop=c == KD - 1, skip_group_check=True)
                last.then_inc(S["gu_psum"], 1)
                pe.wait_ge(S["he_ready"], n * 2 + (h + 1))
                pe.wait_ge(w_full[3 * h + 2], n * 16 + (16 * used[3 * h + 2] + 16))
                for j in range(JE):
                    for gg in range(4):
                        o = D * j + 256 * gg
                        last = mm(PS[32 * gg:32 * gg + 32, 4 + h, 0:256], hTe[:, h, j, :],
                                  slots[:, 3 * h + 2, o:o + 256], start=j == 0, stop=j == JE - 1, skip_group_check=True)
                last.then_inc(S["ye_psum"], 1)

            with pe.Fori(0, PAIRS) as it:
                for h in range(2):
                    expert(it, h)
            extra = pe.value_load(extra_i[0:1, 0:1], min_val=0, max_val=SWEEPS - 1)
            with pe.If(extra > 0):
                with pe.Fori(0, extra) as r:
                    with pe.Fori(0, PAIRS) as it:
                        for h in range(2):
                            expert(r * PAIRS + it + PAIRS, h)

            pe.wait_ge(S["hn_ready"], 1)
            for c in range(KD):
                last = pe.transpose(PS[:, 0, META * c:META * c + META], hnrow[0:META, 0, P * c:P * c + P], ident[0:META, 0:META])
            last.then_inc(S["hnT_psum"], 1)
            for n in range(4):
                t, h = n // 2, n % 2
                pe.wait_ge(S["hn_ready"], 2 + t)
                transposes(1 + n, [hnrow[:, 1 - t, P * c:P * c + P] for c in range(4 * h, 4 * h + 4)])\
                    .then_inc(S["hnT_psum"], 1)
            pe.wait_ge(S["hnT_ready"], 1)

            def block_T(bank, w, col, rhs, n, off=0, start=True):
                for c in range(KD):
                    last = mm(PS[:, bank, off:off + n], w[:, c, col:col + P], rhs(c), start=c == 0, stop=c == KD - 1,
                              skip_group_check=True)
                return last

            def x_of(c):
                return hnT[:, c, META:LK]

            def all_of(c):
                return hnT[:, c, :]

            for n in range(2 * RH):
                name, h = ("rq" if n < RH else "rk"), n % RH
                chunk2_landed(pe, name, h // 2)
                w = chunk2(name, h // 2)
                if n >= 2:
                    pe.wait_ge(S["rot_done"], n - 1)
                for i in range(2):
                    last = block_T(2 * (n % 2) + i, w, 256 * (h % 2) + P * i, x_of if n < RH else all_of,
                                   TOK if n < RH else LK)
                last.then_inc(S["rqk_psum"], 1)
            for h in range(RH):
                pe.wait_ge(S["rot_done"], RH + h + 1)
                if h >= 2:
                    pe.wait_ge(S["rs_ready"], h - 1)
                for bank, keys, m, q0, off in ((4 + h % 2, META, P, 0, 0), (4 + h % 2, META + P, P, P, TOK),
                                               (6 + h % 2, 0, META, 0, 0)):
                    for d in range(2):
                        last = mm(PS[0:m, bank, off:off + TOK - q0], kR[:, 2 * h + d, keys:keys + m], qR[:, 2 * h + d, q0:TOK],
                                  start=d == 0, stop=d == 1, skip_group_check=True)
                last.then_inc(S["rs_psum"], 1)

            def ret_T(h, t):
                k = TT * h + t
                pe.wait_ge(S["yr_ready"], h + 1)
                if k >= 1:
                    pe.wait_ge(S["yrT_evac"], k)
                transposes(7, [yr[:, h % 2, t, P * b:P * b + P] for b in range(4)]).then_inc(S["yrT_psum"], 1)

            def value_rows(name, i, banks):
                chunk2_landed(pe, name, i)
                w = chunk2(name, i)
                for b, (lo, m) in zip(banks, ((META, P), (META + P, P), (0, META))):
                    last = rows_of(b, w, lambda c: hnT[:, c, lo:lo + m], CW, 0, m)
                return last

            pe.wait_ge(S["rs_ready"], RH)
            for h in range(RH):
                if h >= 1:
                    pe.wait_ge(S["v_evac"], h)
                value_rows("rv", h, (0, 1, 2)).then_inc(S["v_psum"], 1)
                if h >= 1:
                    ret_T(h - 1, 0)
                    pe.wait_ge(S["rg_silu"], h)
                chunk2_landed(pe, "rg", h)
                for t in range(TT):
                    last = rows_of(3 + t, chunk2("rg", h), lambda c: hnT[:, c, META + P * t:META + P * t + P], CW)
                last.then_inc(S["rg_psum"], 1)
                if h >= 1:
                    ret_T(h - 1, 1)
                pe.wait_ge(S["v_evac"], h + 1)
                for t in range(TT):
                    mm(PS[:, 5 + t, :], sTm[0:META, h, P * t:P * t + P], vmbuf[0:META, h % 2, :], start=True, stop=False)
                    last = mm(PS[:, 5 + t, :], sT[:, h, P * t:P * t + P], vbuf[:, h % 2, 0, :], start=False, stop=t == 0)
                last = mm(PS[:, 6, :], sT[:, h, TOK:DIAG], vbuf[:, h % 2, 1, :], start=False, stop=True)
                last.then_inc(S["y_psum"], 1)
            for t in range(TT):
                ret_T(RH - 1, t)

            for m in range(2 * KD):
                name, j = ("sq" if m < KD else "sk"), m % KD
                if j % 4 == 0:
                    chunk2_landed(pe, name, j // 4)
                if m >= 4:
                    pe.wait_ge(S["sqk_evac"], m - 3)
                block_T(m % 4, chunk2(name, j // 4), P * (j % 4), x_of if m < KD else all_of, TOK if m < KD else LK)\
                    .then_inc(S["sqk_psum"], 1)
            for i in range(2):
                if i == 1:
                    pe.wait_ge(S["sv_evac"], 1)
                value_rows("sv", i, (4, 5, 6)).then_inc(S["sv_psum"], 1)

            def sb_z(n):
                h, b = SB_ORDER[n], SB_BANKS[n % 4]
                r, m = 64 * (h % 2), h // 2
                if n >= 4:
                    pe.wait_ge(S["arg_done"], n - 3)
                mm(PS[:, b, 0:TOK], kR[r:r + 64, m, META:META + P], qR[r:r + 64, m, :], start=True, stop=False,
                   skip_group_check=True)
                mm(PS[:, b, TOK:DIAG], kR[r:r + 64, m, META + P:LK], qR[r:r + 64, m, P:TOK], start=False, stop=False,
                   skip_group_check=True).then_inc(S["z_psum"], 1)

            def sb_meta_z(G):
                for gg in range(4):
                    h = SB_ORDER[4 * G + gg]
                    r, m = 64 * (h % 2), h // 2
                    last = mm(PS[32 * gg:32 * gg + 32, 3 + G % 2, 0:TOK], kR[r:r + 64, m, 0:32], qR[r:r + 64, m, :],
                              start=True, stop=False, skip_group_check=True)
                last.then_inc(S["mz_psum"], 1)

            def sb_cum(n):
                G, gg, b, L = n // 4, n % 4, SB_BANKS[n % 4], EL[:, n % 3, :]
                bm = 3 + G % 2
                rows = slice(32 * gg, 32 * gg + 32)
                pe.wait_ge(S["L_ready"], n + 1)
                pe.wait_ge(S["Lm_ready"], G + 1)
                mm(PS[:, b, 0:DIAG], K2["negtri"], L, start=False, stop=False, skip_group_check=True)
                mm(PS[:, b, P:TOK], K2["negones"], L[:, TOK:DIAG], start=False, stop=True, skip_group_check=True)
                mm(PS[rows, bm, 0:TOK], K2["negones"][:, 0:32], L[:, 0:TOK], start=False, stop=False, skip_group_check=True)
                mm(PS[rows, bm, P:TOK], K2["negones"][:, 0:32], L[:, TOK:DIAG], start=False, stop=False, skip_group_check=True)
                own = slice(32 * gg, 32 * gg + META)
                mm(PS[rows, bm, 0:TOK], K2["negtri"][own, rows], Lm[own, :], start=False, stop=True, skip_group_check=True,
                   tile_position=(32 * gg, 32 * gg)).then_inc(S["cum_psum"], 1)

            def sb_values(G):
                pe.wait_ge(S["aT_ready"], 4 * G + 4)
                pe.wait_ge(S["aTm_ready"], G + 1)
                pe.wait_ge(S["vm_copied"], 48)
                if G >= 2:
                    pe.wait_ge(S["ysb_evac"], G - 1)
                for gg in range(4):
                    n = 4 * G + gg
                    h = SB_ORDER[n]
                    o = TOK * (gg % 2)
                    dst = PS[64 * (h % 2):64 * (h % 2) + 64, 5 + gg // 2, :]
                    vc = slice(HD * h, HD * h + HD)
                    mm(dst[:, o:o + TOK], vS[:, 0, vc], aT[:, n % 6, 0:TOK], start=True, stop=False, skip_group_check=True)
                    mm(dst[:, o + P:o + TOK], vS[:, 1, vc], aT[:, n % 6, TOK:DIAG], start=False, stop=False, skip_group_check=True)
                    own = slice(32 * gg, 32 * gg + META)
                    if n:
                        pe.wait_ge(S["head_done"], n)
                    mm(dst[:, o:o + TOK], vmS[own, vc], aTm[own, G % 2, :], start=False, stop=True, skip_group_check=True,
                       tile_position=(32 * gg, 64 * (h % 2))).then_inc(S["head_done"], 1)

            pe.wait_ge(S["sqk_evac"], 2 * KD)
            pe.wait_ge(S["sv_evac"], 2)
            pe.wait_ge(S["yrT_evac"], TT * RH)
            sb_meta_z(0)
            sb_z(0)
            sb_z(1)
            for n in range(SH):
                if n + 2 < SH:
                    if (n + 2) % 4 == 0:
                        sb_meta_z((n + 2) // 4)
                    sb_z(n + 2)
                sb_cum(n)
                if n % 4 == 0 and n:
                    sb_values(n // 4 - 1)
            sb_values(3)

            for q in range(4):
                half, b = q % 2, 4 * (q % 2)
                src, parts = (yrT, 16) if q < 2 else (ysbT, KD)
                if q == 0:
                    pe.wait_ge(S["aTm_ready"], 4)
                if q == 1:
                    pe.wait_ge(S["ysb_evac"], 4)
                if q >= 2:
                    pe.wait_ge(S["merge_done"], q - 1)
                for i in range(4):
                    if q < 2:
                        name, ci, col = "ro", 2 * half + i // 2, P * (i % 2)
                    else:
                        name, ci, col = "so", half, P * i
                    if col == 0:
                        chunk2_landed(pe, name, ci)
                    w = chunk2(name, ci)
                    for c in range(parts):
                        last = mm(PS[:, b + i // 2, TOK * (i % 2):TOK * (i % 2) + TOK], w[:, c, col:col + P], src[:, c, :],
                                  start=c == 0, stop=c == parts - 1, skip_group_check=True)
                    if q < 2 and i % 2 == 1:
                        last.then_inc(S["ro_psum"], 1)
                    if q >= 2 and i == 3:
                        last.then_inc(S["so_psum"], 1)
                name = "ga" if q < 2 else "gb"
                chunk2_landed(pe, name, half)
                for i in range(4):
                    last = block_T(b + 2 + i // 2, chunk2(name, half), P * i, x_of, TOK, TOK * (i % 2))
                last.then_inc(S["quad_psum"], 1)

            pe.wait_ge(S["merge_done"], 4)
            for o in range(2):
                chunk2_landed(pe, "o2", o)
                for t in range(TT):
                    last = rows_of(2 * t + o, chunk2("o2", o), lambda c: merged[:, c, P * t:P * t + P], CW)
                last.then_inc(S["mix_psum"], 1)
            for n in range(4):
                t, h = n // 2, n % 2
                pe.wait_ge(S["hn_ready"], 4 + t)
                transposes(4 + n, [hnrow[:, t, P * c:P * c + P] for c in range(4 * h, 4 * h + 4)]).then_inc(S["hnT_psum"], 1)
            pe.wait_ge(S["hnT_ready"], 2)
            for j in range(FB // 2):
                chunk2_landed(pe, "fi", j)
                w = chunk2("fi", j)
                if j >= 2:
                    pe.wait_ge(S["ff_ready"], j - 1)
                for u in range(2):
                    for i in range(2):
                        for c in range(KD):
                            last = mm(PS[:, 2 * (j % 2) + u, TOK * i:TOK * i + TOK], w[:, c, u, P * i:P * i + P],
                                      hnT[:, c, 0:TOK], start=c == 0, stop=c == KD - 1, skip_group_check=True)
                last.then_inc(S["ff_psum"], 1)
            for c in range(FB):
                i = c // 4
                if c % 4 == 0:
                    chunk2_landed(pe, "fo", i)
                pe.wait_ge(S["ff_ready"], c // 2 + 1)
                for t in range(TT):
                    for o in range(2):
                        last = mm(PS[:, 4 + 2 * t + o, :], gT[:, c, P * t:P * t + P], chunk2("fo", i)[:, c % 4, CW * o:CW * o + CW],
                                  start=c == 0, stop=c == FB - 1, skip_group_check=True)
                if c % 4 == 3 or c == FB - 1:
                    last.then_inc(S["fo_psum"], 1)


def shape_constants():
    f = np.float32
    a = np.zeros((P, CA_N), f)
    i = np.arange(P)
    a[:, 0:128] = np.eye(P)
    a[:, 128:256] = 1
    a[:, 256:384] = i[:, None] < i[None, :]
    a[:, 384:512] = (i[:, None] // HD == i[None, :] // HD) / f(HD)
    a[:, 512:544] = np.arange(E)
    a[:, 544:548] = np.arange(EG) + 8
    a[:, 548:552] = np.arange(EG)
    a[:, 552:559] = CAP * np.arange(1, 8)
    tok = np.arange(TOK)
    inv = f(10000.0) ** (-np.arange(0, 32, 2, dtype=f) / f(32))
    ang = np.stack([(tok // 64).astype(f)[:, None] * inv, (tok % 64).astype(f)[:, None] * inv], 1).reshape(TT, P, 32)
    a[:, 568:632] = np.cos(ang).transpose(1, 0, 2).reshape(P, 64)
    a[:, 632:696] = np.sin(ang).transpose(1, 0, 2).reshape(P, 64)
    c = np.zeros((P, CC_N), f)
    inv = f(10000.0) ** (-np.arange(P, dtype=f) / f(P))
    ang = inv[:, None] * np.arange(LK, dtype=f)[None, :]
    c[:, 0:LK], c[:, LK:2 * LK] = np.cos(ang), np.sin(ang)
    c[:, 544:672] = -(i[:, None] >= i[None, :]).astype(f)
    c[:, 672:800] = -1
    c[:, 800:928] = i[:, None] < i[None, :]
    c[:, 928:1312] = 0
    for o in (0, TOK):
        c[:, 928 + o:928 + o + P] = np.where(i[:, None] < i[None, :], 0, -BIG)
    q = np.concatenate([tok, np.arange(P, TOK)])
    key = np.concatenate([np.zeros(TOK, int), np.full(P, P)])[None, :] + i[:, None]
    for h in range(RH):
        log_g = np.log1p(-(2.0 ** (-5.0 - h)))
        diff = q[None, :] - key
        c[:, 1312 + DIAG * h:1312 + DIAG * h + DIAG] = np.where(diff >= 0, np.exp(log_g * np.maximum(diff, 0)), 0) * RDK ** -0.5
        o = 1312 + RH * DIAG + TOK * h
        c[0:META, o:o + TOK] = np.exp(log_g * (META + tok[None, :] - np.arange(META)[:, None])) * RDK ** -0.5
    return {"consts_a": a, "consts_c": c}


_INS = ["x", "c", "ctx", "c_ctx", "w_mod", "b_mod", "norm1_g", "w_in", "q_norm_g", "k_norm_g", "conv_w", "attn_out_g",
        "conv_out_g", "w_out", "norm2_g", "w_group", "w_router", "w_gate", "w_up", "w_down", "final_g", "meta_tokens_2",
        "w_in_2", "w_ret_out_2", "w_sb_out_2", "w_out_2", "w_ffn_in_2", "w_ffn_out_2", "norm_mix_pre_2",
        "norm_mix_post_2", "norm_ffn_pre_2", "norm_ffn_post_2"]
_PER_LAYER = {"w_mod", "w_in", "conv_w", "w_out", "w_group", "w_router", "w_gate", "w_up", "w_down", "w_in_2", "w_ret_out_2",
              "w_sb_out_2", "w_out_2", "w_ffn_in_2", "w_ffn_out_2"}


def kernel(**inputs):
    import concourse.bacc as _bacc
    from concourse.bass_utils import run_bass_kernel_spmd as _run

    nc = _bacc.Bacc("TRN2", target_bir_lowering=False, num_devices=1)
    arrays, aps = {}, {}
    for name, value in [(n, inputs[n]) for n in _INS] + list(shape_constants().items()):
        a = np.ascontiguousarray(value)
        if name in _PER_LAYER:
            a = a.reshape(a.shape[1:])
        if name == "final_g":
            a = a.reshape(1, D)
        arrays[f"in_{name}"] = a
        aps[name] = nc.dram_tensor(f"in_{name}", a.shape, mybir.dt.from_np(a.dtype), kind="ExternalInput").ap()
    out = nc.dram_tensor("out_rows", (TOK, D), F32, kind="ExternalOutput").ap()
    build(nc, aps, out)
    r = _run(nc, [arrays], core_ids=[0])
    return r.results[0]["out_rows"].reshape(1, TOK, D)
```
